# Optimizing a Trainium2 kernel written in Bass

```python
import jax, jax.numpy as jnp
from jax import lax
import numpy as np

D_MODEL = 1024
BATCH = 1
SEQ = 1024
DEPTH = 2
DEC_BATCH = 8
DEC_SEQ = 4
PAST_LEN = 4096
PAGE_SIZE = 128

N_HEADS = 8
NOPE_DIM = 64
ROPE_DIM = 32
V_DIM = 64
Q_LORA = 256
KV_LORA = 128
MLA_WIDTH = N_HEADS * V_DIM
GM_GROUPS = 8
GM_HEAD_DIM = 64
GM_WIDTH = GM_GROUPS * GM_HEAD_DIM
CHUNK = 128
IN_WIDTH = Q_LORA + KV_LORA + ROPE_DIM + 2 * GM_WIDTH
D_FF = 4 * D_MODEL
ROPE_THETA = 10000.0
EPS = 1e-6
Q_BLOCK = 128
ATTN_SCALE = (NOPE_DIM + ROPE_DIM) ** -0.5
NEG_INF = -1e30

kernel_name = "hybrid_mla_chunk_gmlp_decode_step"

def rmsnorm(x, g):
    xf = x.astype(jnp.float32)
    y = xf * lax.rsqrt(jnp.mean(xf * xf, axis=-1, keepdims=True) + EPS)
    return (y * g.astype(jnp.float32)).astype(x.dtype)

def rope(x, pos):
    half = ROPE_DIM // 2
    freqs = ROPE_THETA ** (-jnp.arange(half, dtype=jnp.float32) / half)
    ang = pos.astype(jnp.float32)[:, None] * freqs[None, :]
    cos = jnp.cos(ang)[None, :, None, :]
    sin = jnp.sin(ang)[None, :, None, :]
    x1 = x[..., :half].astype(jnp.float32)
    x2 = x[..., half:].astype(jnp.float32)
    out = jnp.concatenate([x1 * cos - x2 * sin, x2 * cos + x1 * sin], axis=-1)
    return out.astype(x.dtype)

def project(h, pos, w_in, q_norm, w_uq, kv_norm, w_uk, v_norm):
    z = jnp.einsum('btd,de->bte', h, w_in)
    s1 = Q_LORA
    s2 = s1 + KV_LORA
    s3 = s2 + ROPE_DIM
    s4 = s3 + GM_WIDTH
    q_lat, c_kv, k_pe, u, v = jnp.split(z, [s1, s2, s3, s4], axis=-1)
    q = jnp.einsum('btr,rhe->bthe', rmsnorm(q_lat, q_norm), w_uq)
    q_nope, q_pe = q[..., :NOPE_DIM], q[..., NOPE_DIM:]
    q_pe = rope(q_pe, pos)
    q_abs = jnp.einsum('bthn,chn->bthc', q_nope, w_uk)
    c_kv = rmsnorm(c_kv, kv_norm)
    k_pe = rope(k_pe[:, :, None, :], pos)[:, :, 0, :]
    v = rmsnorm(v, v_norm)
    return q_abs, q_pe, c_kv, k_pe, u, v

def latent_attention(q_abs, q_pe, c_kv, k_pe, q_pos, k_pos, w_uv):
    s = (jnp.einsum('bqhc,bkc->bhqk', q_abs, c_kv, preferred_element_type=jnp.float32)
         + jnp.einsum('bqhr,bkr->bhqk', q_pe, k_pe, preferred_element_type=jnp.float32)) * ATTN_SCALE
    mask = k_pos[None, :] <= q_pos[:, None]
    s = jnp.where(mask[None, None], s, NEG_INF)
    p = jax.nn.softmax(s, axis=-1).astype(c_kv.dtype)
    o_lat = jnp.einsum('bhqk,bkc->bqhc', p, c_kv)
    o = jnp.einsum('bqhc,chv->bqhv', o_lat, w_uv)
    return o.reshape(o.shape[0], o.shape[1], MLA_WIDTH)

def prompt_attention(q_abs, q_pe, c_kv, k_pe, w_uv):
    B, T = q_abs.shape[0], q_abs.shape[1]
    nb = T // Q_BLOCK
    qa = q_abs.reshape(B, nb, Q_BLOCK, N_HEADS, KV_LORA).transpose(1, 0, 2, 3, 4)
    qp = q_pe.reshape(B, nb, Q_BLOCK, N_HEADS, ROPE_DIM).transpose(1, 0, 2, 3, 4)
    k_pos = jnp.arange(T, dtype=jnp.int32)

    def one_block(args):
        qa_b, qp_b, i = args
        q_pos = i * Q_BLOCK + jnp.arange(Q_BLOCK, dtype=jnp.int32)
        return latent_attention(qa_b, qp_b, c_kv, k_pe, q_pos, k_pos, w_uv)

    o = lax.map(one_block, (qa, qp, jnp.arange(nb, dtype=jnp.int32)))
    return o.transpose(1, 0, 2, 3).reshape(B, T, MLA_WIDTH)

def chunk_gating(u, v, w_s, b_s):
    B, T = u.shape[0], u.shape[1]
    n_chunks = -(-T // CHUNK)
    pad = n_chunks * CHUNK - T
    vp = jnp.pad(v, ((0, 0), (0, pad), (0, 0))).reshape(B, n_chunks, CHUNK, GM_GROUPS, GM_HEAD_DIM)
    w = w_s * jnp.tril(jnp.ones((CHUNK, CHUNK), dtype=w_s.dtype))
    mixed = jnp.einsum('gij,bnjgd->bnigd', w, vp) + b_s.T[None, None, :, :, None]
    mixed = mixed.reshape(B, n_chunks * CHUNK, GM_WIDTH)[:, :T]
    return u * mixed

def trunk_layer(x, pos, attend, nm_pre, nm_post, w_in, q_norm, w_uq, kv_norm, w_uk, w_uv,
                v_norm, w_s, b_s, w_out, nf_pre, nf_post, w_up, w_down):
    h = rmsnorm(x, nm_pre)
    q_abs, q_pe, c_kv, k_pe, u, v = project(h, pos, w_in, q_norm, w_uq, kv_norm, w_uk, v_norm)
    a_out = attend(q_abs, q_pe, c_kv, k_pe, w_uv)
    g_out = chunk_gating(u, v, w_s, b_s)
    mix = jnp.einsum('bte,ed->btd', jnp.concatenate([a_out, g_out], axis=-1), w_out)
    x = x + rmsnorm(mix, nm_post)
    hf = jnp.einsum('btd,df->btf', rmsnorm(x, nf_pre), w_up)
    f = jnp.einsum('btf,fd->btd', jnp.square(jax.nn.relu(hf)), w_down)
    x = x + rmsnorm(f, nf_post)
    return x, c_kv, k_pe, v

def setup_inputs(seed: int = 0) -> dict:
    key = jax.random.key(seed)
    ks = jax.random.split(key, 24)
    n_pages = PAST_LEN // PAGE_SIZE
    n_phys = (DEC_BATCH * n_pages * 5) // 4
    f32 = jnp.float32

    def nrm(k, shape, scale=1.0):
        return jax.random.normal(k, shape, f32) * scale

    def gain(k, shape):
        return 1.0 + 0.1 * jax.random.normal(k, shape, f32)

    page_table = jax.random.permutation(ks[4], n_phys)[:DEC_BATCH * n_pages]
    page_table = page_table.reshape(DEC_BATCH, n_pages).astype(jnp.int32)
    return {
        "x_prompt": nrm(ks[0], (BATCH, SEQ, D_MODEL)),
        "x_sample": nrm(ks[1], (DEC_BATCH, DEC_SEQ, D_MODEL)),
        "cache_kv_latent": nrm(ks[2], (DEPTH, n_phys, PAGE_SIZE, KV_LORA)),
        "cache_k_rope": nrm(ks[3], (DEPTH, n_phys, PAGE_SIZE, ROPE_DIM)),
        "page_table": page_table,
        "norm_mix_pre": gain(ks[5], (DEPTH, D_MODEL)),
        "norm_mix_post": gain(ks[6], (DEPTH, D_MODEL)),
        "w_in": nrm(ks[7], (DEPTH, D_MODEL, IN_WIDTH), D_MODEL ** -0.5),
        "q_norm": gain(ks[8], (DEPTH, Q_LORA)),
        "w_uq": nrm(ks[9], (DEPTH, Q_LORA, N_HEADS, NOPE_DIM + ROPE_DIM), Q_LORA ** -0.5),
        "kv_norm": gain(ks[10], (DEPTH, KV_LORA)),
        "w_uk": nrm(ks[11], (DEPTH, KV_LORA, N_HEADS, NOPE_DIM), KV_LORA ** -0.5),
        "w_uv": nrm(ks[12], (DEPTH, KV_LORA, N_HEADS, V_DIM), KV_LORA ** -0.5),
        "v_norm": gain(ks[13], (DEPTH, GM_WIDTH)),
        "w_spatial": nrm(ks[14], (DEPTH, GM_GROUPS, CHUNK, CHUNK), CHUNK ** -0.5),
        "b_spatial": gain(ks[15], (DEPTH, GM_GROUPS, CHUNK)),
        "w_out": nrm(ks[16], (DEPTH, MLA_WIDTH + GM_WIDTH, D_MODEL), (MLA_WIDTH + GM_WIDTH) ** -0.5),
        "norm_ffn_pre": gain(ks[17], (DEPTH, D_MODEL)),
        "norm_ffn_post": gain(ks[18], (DEPTH, D_MODEL)),
        "w_ff_up": nrm(ks[19], (DEPTH, D_MODEL, D_FF), D_MODEL ** -0.5),
        "w_ff_down": nrm(ks[20], (DEPTH, D_FF, D_MODEL), D_FF ** -0.5),
    }

def reference(x_prompt, x_sample, cache_kv_latent, cache_k_rope, page_table,
              norm_mix_pre, norm_mix_post, w_in, q_norm, w_uq, kv_norm, w_uk, w_uv,
              v_norm, w_spatial, b_spatial, w_out, norm_ffn_pre, norm_ffn_post,
              w_ff_up, w_ff_down):
    B, T = x_prompt.shape[0], x_prompt.shape[1]
    DB, DT = x_sample.shape[0], x_sample.shape[1]
    past_len = page_table.shape[1] * PAGE_SIZE
    pos_prompt = jnp.arange(T, dtype=jnp.int32)
    pos_sample = past_len + jnp.arange(DT, dtype=jnp.int32)

    xp, xs = x_prompt, x_sample
    ckv_p, kpe_p, ckv_s, kpe_s, v_s = [], [], [], [], []
    for l in range(DEPTH):
        weights = (norm_mix_pre[l], norm_mix_post[l], w_in[l], q_norm[l], w_uq[l], kv_norm[l],
                   w_uk[l], w_uv[l], v_norm[l], w_spatial[l], b_spatial[l], w_out[l],
                   norm_ffn_pre[l], norm_ffn_post[l], w_ff_up[l], w_ff_down[l])

        xp, c_p, k_p, _ = trunk_layer(xp, pos_prompt, prompt_attention, *weights)

        past_c = cache_kv_latent[l][page_table].reshape(DB, past_len, KV_LORA)
        past_k = cache_k_rope[l][page_table].reshape(DB, past_len, ROPE_DIM)
        k_pos = jnp.arange(past_len + DT, dtype=jnp.int32)

        def sample_attention(q_abs, q_pe, c_kv, k_pe, w_uv_l, past_c=past_c, past_k=past_k, k_pos=k_pos):
            keys_c = jnp.concatenate([past_c, c_kv], axis=1)
            keys_k = jnp.concatenate([past_k, k_pe], axis=1)
            return latent_attention(q_abs, q_pe, keys_c, keys_k, pos_sample, k_pos, w_uv_l)

        xs, c_s, k_s, vrows = trunk_layer(xs, pos_sample, sample_attention, *weights)

        ckv_p.append(c_p.reshape(B, T // PAGE_SIZE, PAGE_SIZE, KV_LORA))
        kpe_p.append(k_p.reshape(B, T // PAGE_SIZE, PAGE_SIZE, ROPE_DIM))
        ckv_s.append(c_s)
        kpe_s.append(k_s)
        v_s.append(vrows)

    new_kv_latent_prompt = jnp.stack(ckv_p, axis=0)
    new_k_rope_prompt = jnp.stack(kpe_p, axis=0)
    new_kv_latent_sample = jnp.stack(ckv_s, axis=0)
    new_k_rope_sample = jnp.stack(kpe_s, axis=0)
    new_chunk_v_sample = jnp.stack(v_s, axis=0)
    return (xp, xs, new_kv_latent_prompt, new_k_rope_prompt, new_kv_latent_sample, new_k_rope_sample, new_chunk_v_sample)


_drawn_inputs = setup_inputs


def setup_inputs(seed=0):
    import zlib

    import numpy as np

    out = dict(_drawn_inputs(seed))
    spreads = {}
    factors = {'cache_k_rope': 4.425, 'q_norm': 5.904}
    for name, (base, spread) in spreads.items():
        noise = np.random.default_rng([zlib.crc32(name.encode()), seed]).standard_normal(out[name].shape)
        drawn = base * np.exp(spread * noise) if base else spread * noise
        out[name] = __import__('jax').numpy.asarray(drawn.astype(out[name].dtype))
    for name, factor in factors.items():
        out[name] = (out[name] * factor).astype(out[name].dtype)
    return out
```

```python
from contextlib import ExitStack

import numpy as np

import concourse.bass as bass
from concourse import mybir

F32 = mybir.dt.float32
F32R = mybir.dt.float32r
I32 = mybir.dt.int32
ALU = mybir.AluOpType
ACT = mybir.ActivationFunctionType
AX = mybir.AxisListType

P = 128
D = 1024
KD = D // P
DEPTH = 2
SEQ = 1024
DB, DT = 8, 4
NS = DB * DT
TOK = SEQ + NS
NG, GW = 3, TOK // 3
NB = SEQ // P
HEADS, NOPE, ROPE, VD = 8, 64, 32, 64
QL, CL = 256, 128
GM = 512
GROUPS = 8
FF = 4096
FB = 8
PAST, PAGE = 4096, 128
PAGES = PAST // PAGE
N_PHYS = DB * PAGES * 5 // 4
SCALE = float((NOPE + ROPE) ** -0.5)
NEG = -1e30
EPS = 1e-6
TW = 1024

Z_Q, Z_C, Z_K, Z_U, Z_V, NZ = 0, 2, 3, 4, 8, 12
UNITS_IN, UNITS_UV, UNITS_OUT, UNITS_UP, UNITS_DOWN = NZ, 4, KD, 4, KD
TILES_LAYER = NZ + KD + FB * 8
UNITS_LAYER = UNITS_IN + UNITS_UV + UNITS_OUT + FB * (UNITS_UP + UNITS_DOWN)
G_MIX_PRE, G_MIX_POST, G_FFN_PRE, G_FFN_POST, G_Q, G_C, G_V, NGAIN = 0, 8, 16, 24, 32, 34, 35, 39
C_TRIG, C_ID, C_TRI, C_TRIL, C_NEW, C_WD = 0, TOK, TOK + P, TOK + 2 * P, TOK + 3 * P, TOK + 3 * P + 2 * NS
C_ALL = C_WD + NS
QUADS, QB = DB // 4, 4
CHUNKS = PAST // 512


class Count:

    def __init__(self, sem, per_layer, credit=0):
        self.sem, self.per, self.credit = sem, per_layer, credit


class Pos:

    def __init__(self, layer):
        self.layer, self.k, self.base = layer, {}, []

    def value(self, s, more=0):
        v = self.layer * s.per + (s.credit + self.k.get(s, 0) + more)
        for i, steps in self.base:
            if s in steps:
                v = v + i * steps[s]
        return v

    def step(self, s, n=1):
        self.k[s] = self.k.get(s, 0) + n

    def enter(self, i, steps):
        self.base.append((i, steps))
        self.at = dict(self.k)

    def leave(self, trips):
        _, steps = self.base.pop()
        for s in set(self.k) | set(steps):
            got = self.k.get(s, 0) - self.at.get(s, 0)
            assert got == steps.get(s, 0), (s.sem, got, steps.get(s, 0))
            self.k[s] = self.at.get(s, 0) + trips * got

    def done(self):
        for s, n in self.k.items():
            assert n <= s.per, (s.sem, n, s.per)


def build(nc, xT, wst, gains, wuq, wuk, wuv, wsp, bsp, cache_c, cache_k, pages, consts,
          yT, o_cp, o_kp, o_cs, o_ks, o_vs, x_spill):
    with ExitStack() as ctx:
        def sb(name, shape, dt=F32):
            return ctx.enter_context(nc.sbuf_tensor(name, shape, dt))

        def sem(name):
            return ctx.enter_context(nc.semaphore(name))

        with nc.sbuf_tensor("x2", [P, KD, TOK], F32) as x2:
            pass
        hh = sb("hh", [P, KD, TOK], F32R)
        hl = sb("hl", [P, KD, TOK], F32R)
        with nc.sbuf_tensor("x", [P, KD, TOK], F32) as x:
            pass
        with nc.sbuf_tensor("scratch", [P, KD * TOK], F32) as scr:
            pass
        hidh = sb("hidh", [P, 4, TOK], F32R)
        hidl = sb("hidl", [P, 4, TOK], F32R)
        z = sb("z", [P, NZ, TOK])
        raw = sb("raw", [P, 2, TW])
        wh = sb("wh", [P, 2, TW], F32R)
        wl = sb("wl", [P, 2, TW], F32R)
        t0 = sb("t0", [P, TOK])
        t1 = sb("t1", [P, TOK])
        rinv = sb("rinv", [P, TOK])
        sacc = sb("sacc", [P, TOK])
        cst = sb("cst", [P, C_ALL])
        cn = sb("cn", [P, NB + 1, CL + ROPE])
        gn = sb("gn", [P, NGAIN])
        ones = sb("ones", [P, P])
        eps = sb("eps", [P, 1])
        stat = sb("stat", [P, 32])
        kpt = sb("kpt", [1, DB * PAGES], I32)

        trig = cst[:, C_TRIG:C_TRIG + TOK]
        ident = cst[:, C_ID:C_ID + P]
        tri = cst[:, C_TRI:C_TRI + P]
        tril = cst[:, C_TRIL:C_TRIL + P]
        tmp = [t0, t1]

        ws = scr[:, 0:1024].rearrange("p (g i) -> p g i", g=GROUPS)
        bb = scr[:, 1024:1536].rearrange("p (a i) -> p a i", a=4)
        wd = scr[0:NS, 1536:1792].rearrange("p (g i) -> p g i", g=GROUPS)
        vn = scr[:, 1792:2816].rearrange("p (b n) -> p b n", b=2)
        gt = scr[:, 2816:3328].rearrange("p (a i) -> p a i", a=4)
        qd = scr[:, 0:1280].rearrange("p (q n) -> p q n", q=QUADS)
        qrd = scr[:, 1280:1536].rearrange("p (q n) -> p q n", q=QUADS)
        qr = scr[0:ROPE, 1536:1792].rearrange("p (q b n) -> p q b n", q=QUADS, b=QB)
        pt = scr[:, 1792:1792 + 4096].rearrange("p (k n) -> p k n", k=NB)
        pr = scr[:, 5888:5888 + 2048].rearrange("p (b n) -> p b n", b=2)
        wq = scr[:, 7936:8448].rearrange("p (h k n) -> p h k n", h=2, k=2)
        ck = scr[:, 1792:1792 + 4096].rearrange("p (s b r c) -> p s b r c", s=2, b=QB, r=4)
        rk = scr[:, 5888:5888 + 1024].rearrange("p (s b r c) -> p s b r c", s=2, b=QB, r=4)
        rk2 = scr[:, 7936:8448].rearrange("p (r b c) -> p r b c", r=4, b=QB)
        wv = scr[:, 6912:7936].rearrange("p (h n) -> p h n", h=HEADS)
        wk = sb("wk", [NOPE, 2, CL])
        qn, qa, qp, rt = t0, t1, rinv, sacc
        ctt = [t0[:, 0:512], t0[:, 512:1024], t1[:, 0:512], t1[:, 512:1024]]
        rtt = sacc[:, 0:512]
        pd = rinv[:, 0:512]
        ptd = rinv[:, 512:1024].rearrange("p (r n) -> p r n", r=4)
        oacc = sacc[:, 512:640]
        kn = sacc[:, 640:672]

        ps = [ctx.enter_context(nc.psum_tensor(f"ps{i}", [P, 512], F32)) for i in range(8)]

        S = {}

        def count(name, per, credit=0):
            S[name] = Count(sem(name), per, credit)
            return S[name]

        raw_in = [count(f"raw_in{i}", 16 * TILES_LAYER // 2) for i in range(2)]
        split = count("split", TILES_LAYER, 2)
        wfree = count("wfree", TILES_LAYER, 2)
        acc_full = count("acc_full", UNITS_LAYER)
        acc_free = count("acc_free", UNITS_LAYER, 2)
        x_new = count("x_new", 2 * KD, KD)
        hh_new = count("hh_new", 2 * KD)
        hl_new = count("hl_new", 2 * KD)
        SQ_TILES = 8 + 2 + 1 + 4 + 8 + 8 + 8
        sq_full = count("sq_full", SQ_TILES)
        sq_free = count("sq_free", SQ_TILES, 2)
        sum_full = count("sum_full", 7)
        mean_full = count("mean_full", 21)
        root_full = count("root_full", 21)
        r_full = count("r_full", 7)
        z_done = count("z_done", 1)
        zn_done = count("zn_done", 4)
        x_stored = count("x_stored", 32)
        x_loaded = count("x_loaded", 32)
        s_first = sem("first_loads")
        small_in = count("small_in", 16)
        gate_in = count("gate_in", 16 * (2 + DB))
        wd_zero = count("wd_zero", 1)
        ws_ready = count("ws_ready", 1)
        ct_full = count("ct_full", NB + 1)
        ct_free = count("ct_free", NB + 1)
        vt_full = count("vt_full", NB + 1)
        vt_free = count("vt_free", NB + 1)
        mix_full = count("mix_full", NB + 1)
        mix_free = count("mix_free", NB + 1)
        gateh = count("gateh", 1)
        gate_done = count("gate_done", 1)
        outs = count("outs", 16 * 5)
        qd_zero = count("qd_zero", 1)
        wqk_in = count("wqk_in", 16 * 2 * 4)
        q_full = count("q_full", 3 * HEADS)
        qn_new = count("qn_new", 3 * HEADS)
        qp_new = count("qp_new", 3 * HEADS)
        abs_full = count("abs_full", 3 * HEADS)
        qa_new = count("qa_new", 3 * HEADS)
        s_full = count("s_full", NB * HEADS)
        nmax = count("nmax", NB * HEADS)
        exped = count("exped", NB * HEADS)
        p_new = count("p_new", NB * HEADS)
        pt_full = count("pt_full", 12 * HEADS)
        pt_new = count("pt_new", 12 * HEADS)
        o_full = count("o_full", 2 * HEADS)
        o_new = count("o_new", 2 * HEADS)
        qrd_new = count("qrd_new", 1)
        n_step = QUADS * CHUNKS
        cache_in = [count(f"cache_in{i}", 16 * 2 * 16 * n_step // 2) for i in range(2)]
        rk_new = count("rk_new", n_step)
        cache_free = count("cache_free", n_step)
        wv_zero = count("wv_zero", 1)
        wv_in = count("wv_in", 32)
        dct_full = count("dct_full", 5 * n_step)
        dct_act = count("dct_act", 2 * n_step)
        dct_dve = count("dct_dve", 3 * n_step)
        ds_full = count("ds_full", n_step + QUADS)
        dmax = count("dmax", n_step + QUADS)
        dexp = count("dexp", n_step + QUADS)
        dpt_full = count("dpt_full", n_step + QUADS)
        dpt_new = count("dpt_new", n_step + QUADS)
        do_full = count("do_full", n_step + QUADS)
        do_free = count("do_free", n_step + QUADS)
        kn_new = count("kn_new", 1)
        on_new = count("on_new", QUADS)
        ot_full = count("ot_full", QUADS)
        ol_new = count("ol_new", QUADS)
        ab_h = count("ab_h", UNITS_UV)
        ab_l = count("ab_l", UNITS_UV)
        y_new = count("y_new", UNITS_OUT + 1)
        act_new = count("act_new", 4 * FB)
        sq2 = count("sq2", 4 * FB)
        hid_h = count("hid_h", 4 * FB)
        hid_l = count("hid_l", 4 * FB)
        s_init = sem("init")
        s_out = sem("written")

        block = ctx.enter_context(nc.Block())

        def groups(ap):
            return ap.rearrange("p (g n) -> p g n", g=NG)

        def bank3(u, g):
            return ps[3 * (u % 2) + g][:, 0:GW]

        def cols(g):
            return slice(g * GW, (g + 1) * GW)

        @block.sync
        def _(sp):
            sp.dma_start(x[:, :, :], xT.rearrange("k p t -> p k t")).then_inc(s_first, 16)
            sp.dma_start(cst[:, :], consts).then_inc(s_first, 16)
            sp.dma_start(kpt[:, :], pages).then_inc(s_first, 16)
            sp.wait_ge(s_first, 48)
            with sp.Fori(0, DEPTH) as l:
                at = Pos(l)

                def tile_in(t):
                    sp.wait_ge(split.sem, at.value(split, -1))
                    at.step(split)
                    sl = raw_in[t % 2]
                    sp.dma_start(raw[:, t % 2, :], wst[l, t]).then_inc(sl.sem, 16)

                sp.wait_ge(x_new.sem, at.value(x_new))
                sp.dma_start(gn[:, :], gains[l]).then_inc(small_in.sem, 16)
                for t in range(2):
                    tile_in(t)
                sp.dma_start(x_spill.rearrange("k p t -> p k t"), x[:, :, :]).then_inc(x_stored.sem, 16)
                for t in range(2, NZ):
                    tile_in(t)
                at.step(x_stored, 16)
                sp.wait_ge(x_stored.sem, at.value(x_stored))
                at.step(hl_new, KD)
                sp.wait_ge(hl_new.sem, at.value(hl_new))
                sp.dma_start(ws, wsp[l]).then_inc(gate_in.sem, 16)
                sp.dma_start(bb, bsp[l]).then_inc(gate_in.sem, 16)
                at.step(wd_zero)
                sp.wait_ge(wd_zero.sem, at.value(wd_zero))
                for b in range(DB):
                    sp.dma_start(wd[DT * b:DT * b + DT, :, DT * b:DT * b + DT],
                                 wsp[l][0:DT, :, 0:DT]).then_inc(gate_in.sem, 16)
                for t in range(NZ, NZ + 2):
                    tile_in(t)
                at.step(ct_free, NB + 1)
                sp.wait_ge(ct_free.sem, at.value(ct_free))
                sp.dma_start(o_cp[l].rearrange("n p c -> p n c"), cn[:, 0:NB, 0:CL]).then_inc(outs.sem, 16)
                sp.dma_start(o_kp[l].rearrange("n p c -> p n c"), cn[:, 0:NB, CL:]).then_inc(outs.sem, 16)
                sp.dma_start(o_cs[l], cn[0:NS, NB, 0:CL]).then_inc(outs.sem, 16)
                sp.dma_start(o_ks[l], cn[0:NS, NB, CL:]).then_inc(outs.sem, 16)
                at.step(vt_free, NB + 1)
                sp.wait_ge(vt_free.sem, at.value(vt_free))
                sp.dma_start(o_vs[l], vn[0:NS, NB % 2, :]).then_inc(outs.sem, 16)
                at.step(wv_zero)
                sp.wait_ge(wv_zero.sem, at.value(wv_zero))
                for e in range(2):
                    dst = wv.rearrange("p (a e) n -> p a e n", e=2)[:, :, e, VD * e:VD * e + VD]
                    src = wuv[l].rearrange("c (a e) v -> c a e v", e=2)[:, :, e, :]
                    sp.dma_start(dst, src).then_inc(wv_in.sem, 16)

                def gather(quad, c, s, first):
                    free = None if first else sp.snap(at.value(cache_free, -1))
                    at.step(cache_free)
                    for b in range(QB):
                        for i in range(4):
                            pg = sp.value_load(kpt[0:1, bass.ds(c * 4 + ((quad * QB + b) * PAGES + i), 1)],
                                               min_val=0, max_val=N_PHYS - 1)
                            row = sp.snap(l * N_PHYS + pg)
                            if b == 0 and i == 0 and not first:
                                sp.wait_ge(cache_free.sem, free)
                            sp.dma_start(ck[32 * i:32 * i + 32, s, b, :, :], cache_c[row]).then_inc(cache_in[s].sem, 16)
                            sp.dma_start(rk[32 * i:32 * i + 32, s, b, :, :], cache_k[row]).then_inc(cache_in[s].sem, 16)

                for quad in range(QUADS):
                    for s in range(2):
                        gather(quad, s, s, quad == 0)
                    with sp.Fori(1, CHUNKS // 2) as i:
                        at.enter(i - 1, {cache_free: 2})
                        for s in range(2):
                            gather(quad, i * 2 + s, s, False)
                        at.leave(CHUNKS // 2 - 1)
                at.step(ab_l, UNITS_UV)
                sp.wait_ge(ab_l.sem, at.value(ab_l))
                sp.dma_start(x[:, :, :], x_spill.rearrange("k p t -> p k t")).then_inc(x_loaded.sem, 16)
                for t in range(NZ + 2, NZ + KD + 2):
                    tile_in(t)
                at.step(x_new, KD)
                sp.wait_ge(x_new.sem, at.value(x_new))
                sp.dma_start(x_spill.rearrange("k p t -> p k t"), x[:, :, :]).then_inc(x_stored.sem, 16)
                base = NZ + KD + 2
                with sp.Fori(0, FB - 1) as i:
                    at.enter(i, {split: 8})
                    for t in range(8):
                        sp.wait_ge(split.sem, at.value(split, -1))
                        at.step(split)
                        sp.dma_start(raw[:, t % 2, :], wst[l, i * 8 + (base + t)]).then_inc(raw_in[t % 2].sem, 16)
                    at.leave(FB - 1)
                for t in range(base + (FB - 1) * 8, TILES_LAYER):
                    tile_in(t)
                at.step(acc_full, UNITS_LAYER - KD)
                sp.wait_ge(acc_full.sem, at.value(acc_full))
                at.step(acc_full, KD)
                at.step(x_stored, 16)
                sp.dma_start(x2[:, :, :], x_spill.rearrange("k p t -> p k t")).then_inc(x_loaded.sem, 16)
                at.step(x_new, KD)
                at.step(hl_new, KD)
                at.done()
            sp.wait_ge(x_new.sem, x_new.credit + DEPTH * x_new.per)
            sp.dma_start(yT.rearrange("k p t -> p k t"), x[:, :, :]).then_inc(s_out, 16)
            sp.wait_ge(s_out, 16)
            sp.wait_ge(outs.sem, DEPTH * outs.per)
            sp.wait_ge(x_stored.sem, DEPTH * x_stored.per)

        @block.gpsimd
        def _(pool):
            pool.memset(ones[:, :], 1.0).then_inc(s_init, 1)
            pool.memset(eps[:, :], EPS).then_inc(s_init, 1)
            pool.memset(stat[:, 30:31], 0.0).then_inc(split.sem, 2)
            pool.memset(stat[:, 31:32], 0.0).then_inc(wfree.sem, 2)
            with pool.Fori(0, DEPTH * TILES_LAYER // 2) as i:
                for s in range(2):
                    pool.wait_ge(raw_in[s].sem, i * 16 + 16)
                    pool.wait_ge(wfree.sem, i * 2 + (s + 1))
                    pool.tensor_tensor(wh[:, s, :], raw[:, s, :], ones[:, 0:1].to_broadcast([P, TW]), ALU.mult)
                    pool.drain()
                    pool.tensor_tensor(wl[:, s, :], raw[:, s, :], wh[:, s, :].bitcast(F32),
                                       ALU.subtract).then_inc(split.sem, 1)

        @block.scalar
        def _(act):
            act.wait_ge(s_init, 2)
            act.wait_ge(s_first, 48)
            with act.Fori(0, DEPTH) as l:
                at = Pos(l)

                def squares(tiles, ready):
                    for k, t in enumerate(tiles):
                        ready(k)
                        act.wait_ge(sq_free.sem, at.value(sq_free, -1))
                        at.step(sq_free)
                        sl = at.k.get(sq_full, 0) % 2
                        act.activation(tmp[sl][:, :], t, ACT.Square).then_inc(sq_full.sem, 1)
                        at.step(sq_full)

                def roots(n):
                    for g in range(NG):
                        at.step(mean_full)
                        act.wait_ge(mean_full.sem, at.value(mean_full))
                        if g == 0 and at.k.get(r_full, 0):
                            pass
                        act.activation(rinv[:, cols(g)], ps[6 + g % 2][:, 0:GW], ACT.Sqrt,
                                       bias=eps[:, 0:1], scale=1.0 / n).then_inc(root_full.sem, 1)
                        at.step(root_full)

                def new_h(gain):
                    for k in range(KD):
                        act.wait_ge(x_new.sem, at.value(x_new, -KD + k + 1))
                        act.activation(hh[:, k, :], x[:, k, :], ACT.Copy,
                                       scale=gn[:, gain + k:gain + k + 1]).then_inc(hh_new.sem, 1)
                        at.step(hh_new)
                        act.wait_ge(sq_free.sem, at.value(sq_free, -1))
                        at.step(sq_free)
                        sl = at.k.get(sq_full, 0) % 2
                        act.activation(tmp[sl][:, :], x[:, k, :], ACT.Square).then_inc(sq_full.sem, 1)
                        at.step(sq_full)
                    roots(D)

                at.step(small_in, 16)
                act.wait_ge(small_in.sem, at.value(small_in))
                new_h(G_MIX_PRE)
                at.step(z_done)
                act.wait_ge(z_done.sem, at.value(z_done))
                for first, n in ((Z_Q, 2), (Z_C, 1), (Z_V, 4)):
                    squares([z[:, first + k, :] for k in range(n)], lambda k: None)
                    roots(n * P)
                for t in range(NB + 1):
                    m = P if t < NB else NS
                    at.step(ct_full)
                    act.wait_ge(ct_full.sem, at.value(ct_full))
                    act.activation(cn[0:m, t, :], ps[4 + t % 2][0:m, 0:CL + ROPE], ACT.Copy).then_inc(ct_free.sem, 1)
                    at.step(ct_free)
                at.step(x_stored, 16)
                act.wait_ge(x_stored.sem, at.value(x_stored))
                for t in range(NB + 1):
                    m = P if t < NB else NS
                    at.step(vt_full)
                    act.wait_ge(vt_full.sem, at.value(vt_full))
                    if t >= 2:
                        act.wait_ge(mix_full.sem, at.value(mix_full, t - 1))
                    act.activation(vn[0:m, t % 2, :], ps[6 + t % 2][0:m, :], ACT.Copy).then_inc(vt_free.sem, 1)
                    at.step(vt_free)
                at.step(mix_full, NB + 1)
                at.step(mix_free, NB + 1)
                act.wait_ge(mix_free.sem, at.value(mix_free))
                act.activation(hh[:, 4:8, :], z[:, Z_U:Z_U + 4, :], ACT.Copy).then_inc(gateh.sem, 1)
                at.step(gateh)
                at.step(gate_done)
                act.wait_ge(gate_done.sem, at.value(gate_done))
                at.step(outs, 80)
                act.wait_ge(outs.sem, at.value(outs))

                def head(hp, e):
                    for g in range(NG):
                        at.step(q_full)
                        act.wait_ge(q_full.sem, at.value(q_full))
                        act.activation(qn[0:NOPE, cols(g)], ps[g][0:NOPE, 0:GW], ACT.Copy).then_inc(qn_new.sem, 1)
                        at.step(qn_new)
                    for g in range(NG):
                        at.step(abs_full)
                        act.wait_ge(abs_full.sem, at.value(abs_full))
                        act.activation(qa[:, cols(g)], ps[3 + g][:, 0:GW], ACT.Copy).then_inc(qa_new.sem, 1)
                        at.step(qa_new)
                    at.step(qd_zero, 1 if at.k.get(qd_zero, 0) == 0 else 0)
                    act.drain()
                    act.wait_ge(qd_zero.sem, at.value(qd_zero))
                    dst = qd[:, :, :].rearrange("p q (b n) -> p q b n", n=160)[:, :, :, bass.ds(hp * 8 + 4 * e, 4)]
                    act.activation(dst, qa[:, SEQ:TOK].rearrange("p (q b t) -> p q b t", q=QUADS, b=QB), ACT.Copy)

                    def evac_pt(j):
                        for n in range(1 if j < 4 else 2):
                            at.step(pt_full)
                            act.wait_ge(pt_full.sem, at.value(pt_full))
                            kb = min(4, j + 1 - 4 * n)
                            bank = 4 + (at.k[pt_full] - 1) % 2
                            src = ps[bank][:, 0:kb * P].rearrange("p (k n) -> p k n", k=kb)
                            act.activation(pt[:, 4 * n:4 * n + kb, (j % 4) * P:(j % 4 + 1) * P], src,
                                           ACT.Copy).then_inc(pt_new.sem, 1)
                            at.step(pt_new)

                    def evac_o(sb_):
                        at.step(o_full)
                        act.wait_ge(o_full.sem, at.value(o_full))
                        dst = z[:, bass.ds(hp * 2 + (Z_U + e), 1), 512 * sb_:512 * sb_ + 512]
                        act.activation(dst, ps[6][:, :].rearrange("p (a n) -> p a n", a=1),
                                       ACT.Copy).then_inc(o_new.sem, 1)
                        at.step(o_new)

                    for j in range(NB):
                        at.step(nmax)
                        act.wait_ge(nmax.sem, at.value(nmax))
                        n = (j + 1) * P
                        for c in range((n + 511) // 512):
                            w = min(512, n - 512 * c)
                            ins = act.activation(pr[:, j % 2, 512 * c:512 * c + w], ps[2 * (j % 2) + c][:, 0:w],
                                                 ACT.Exp, bias=stat[:, j % 2:j % 2 + 1], scale=SCALE,
                                                 accum_out=stat[:, 2 + 2 * (j % 2) + c:3 + 2 * (j % 2) + c])
                        ins.then_inc(exped.sem, 1)
                        at.step(exped)
                        if j > 0:
                            evac_pt(j - 1)
                        if j == 4:
                            evac_o(0)
                    evac_pt(NB - 1)
                    evac_o(1)

                with act.Fori(0, HEADS // 2) as hp:
                    at.enter(hp, {wqk_in: 32, q_full: 6, qn_new: 6, abs_full: 6, qa_new: 6, nmax: 16, exped: 16,
                                  pt_full: 24, pt_new: 24, o_full: 4, o_new: 4})
                    for k, t in ((1, wq), (2, wk[:, :, :])):
                        if k == 1:
                            act.dma_start(t, wuq[l, hp]).then_inc(wqk_in.sem, 16)
                        else:
                            act.dma_start(t, wuk[l, hp]).then_inc(wqk_in.sem, 16)
                        at.step(wqk_in, 16)
                    z0 = at.k.get(qd_zero, 0)
                    for e in range(2):
                        head(hp, e)
                    at.k[qd_zero] = z0
                    at.leave(HEADS // 2)
                at.step(qd_zero)

                def d_exp(first=False):
                    at.step(dmax)
                    act.wait_ge(dmax.sem, at.value(dmax))
                    s = d_exp.n % 2
                    d_exp.n += 1
                    if not first:
                        act.activation(stat[:, 12 + s:13 + s], stat[:, 8 + (1 - s):9 + (1 - s)], ACT.Exp,
                                       bias=stat[:, 10 + s:11 + s], scale=SCALE)
                    w = NS if first else 512
                    act.activation(pd[:, 0:w], ps[5][:, 0:w], ACT.Exp, bias=stat[:, 10 + s:11 + s], scale=SCALE,
                                   accum_out=stat[:, 14 + s:15 + s]).then_inc(dexp.sem, 1)
                    at.step(dexp)

                def d_keys():
                    for b in (2, 3):
                        at.step(dct_full, 5 if b == 2 else 0)
                        act.wait_ge(dct_full.sem, at.value(dct_full, b - 4))
                        act.activation(ctt[b], ps[b][:, :], ACT.Copy).then_inc(dct_act.sem, 1)
                        at.step(dct_act)

                def d_pt(n):
                    at.step(dpt_full)
                    act.wait_ge(dpt_full.sem, at.value(dpt_full))
                    if n == 1:
                        act.activation(ptd[0:NS, 0, :], ps[6][0:NS, 0:P], ACT.Copy).then_inc(dpt_new.sem, 1)
                    else:
                        act.activation(ptd, ps[6][:, :].rearrange("p (r n) -> p r n", r=4),
                                       ACT.Copy).then_inc(dpt_new.sem, 1)
                    at.step(dpt_new)

                for quad in range(QUADS):
                    d_exp.n = 0
                    d_exp(True)
                    d_pt(1)
                    d_keys()
                    d_exp()
                    with act.Fori(0, CHUNKS // 2 - 1) as i:
                        at.enter(i, {dct_full: 10, dct_act: 4, dmax: 2, dexp: 2, dpt_full: 2, dpt_new: 2})
                        for s in range(2):
                            d_keys()
                            d_pt(4)
                            d_exp()
                        at.leave(CHUNKS // 2 - 1)
                    d_keys()
                    d_pt(4)
                    d_exp()
                    d_pt(4)
                    at.step(ot_full)
                    act.wait_ge(ot_full.sem, at.value(ot_full))
                    dst = z[:, Z_U:Z_U + HEADS, SEQ + 16 * quad:SEQ + 16 * quad + 16].rearrange(
                        "p h (b t) -> p b h t", b=QB)
                    src = ps[6][:, 0:P].rearrange("p (b h t) -> p b h t", b=QB, h=HEADS)
                    for b in range(QB):
                        ins = act.activation(dst[:, b], src[:, b], ACT.Copy)
                    ins.then_inc(ol_new.sem, 1)
                    at.step(ol_new)
                for u in range(UNITS_UV):
                    at.step(acc_full)
                    act.wait_ge(acc_full.sem, at.value(acc_full, UNITS_IN))
                    for g in range(NG):
                        ins = act.activation(hh[:, u, cols(g)], bank3(u, g), ACT.Copy)
                    ins.then_inc(ab_h.sem, 1)
                    at.step(ab_h)
                at.step(acc_full, UNITS_IN)

                for m in range(UNITS_OUT):
                    at.step(acc_full)
                    act.wait_ge(acc_full.sem, at.value(acc_full))
                    act.wait_ge(sq_free.sem, at.value(sq_free, -1))
                    at.step(sq_free)
                    sl = at.k.get(sq_full, 0) % 2
                    for g in range(NG):
                        ins = act.activation(tmp[sl][:, cols(g)], bank3(m, g), ACT.Square)
                    ins.then_inc(sq_full.sem, 1)
                    at.step(sq_full)
                    for g in range(NG):
                        ins = act.activation(z[:, m, cols(g)], bank3(m, g), ACT.Copy)
                    ins.then_inc(acc_free.sem, 1)
                    at.step(acc_free)
                roots(D)
                at.step(x_new, KD)
                new_h(G_FFN_PRE)
                at.step(x_stored, 16)
                act.wait_ge(x_stored.sem, at.value(x_stored))
                with act.Fori(0, FB) as i:
                    at.enter(i, {act_new: 4, sq2: 4, hid_h: 4})
                    for j in range(4):
                        at.step(act_new)
                        act.wait_ge(act_new.sem, at.value(act_new))
                        s = j % 2
                        act.activation(z[:, 10 + s, :], z[:, 8 + s, :], ACT.Square)
                        at.step(sq2)
                        act.drain()
                        act.activation(hidh[:, j, :], z[:, 10 + s, :], ACT.Copy).then_inc(hid_h.sem, 1)
                        at.step(hid_h)
                    at.leave(FB)
                at.step(acc_full, FB * (UNITS_UP + UNITS_DOWN))
                at.step(y_new, UNITS_OUT + 1)
                squares([z[:, k, :] for k in range(KD)],
                        lambda k: act.wait_ge(y_new.sem, at.value(y_new)) if k == 0 else None)
                roots(D)
                at.step(x_new, KD)
                at.k[acc_free] = acc_free.per
                at.done()

        @block.vector
        def _(dve):
            dve.memset(stat[:, 26:27], 0.0).then_inc(acc_free.sem, 2)
            dve.memset(stat[:, 27:28], 0.0).then_inc(sq_free.sem, 2)
            dve.wait_ge(s_first, 48)
            dve.memset(stat[:, 28:29], 0.0).then_inc(x_new.sem, KD)
            with dve.Fori(0, DEPTH) as l:
                at = Pos(l)

                def accumulate(k):
                    sl = at.k.get(sq_full, 0) % 2
                    at.step(sq_full)
                    if k:
                        dve.drain()
                    dve.wait_ge(sq_full.sem, at.value(sq_full))
                    if k == 0:
                        dve.wait_ge(root_full.sem, at.value(root_full)) if at.k.get(root_full, 0) else None
                        ins = dve.tensor_copy(sacc[:, :], tmp[sl][:, :])
                    else:
                        ins = dve.tensor_tensor(sacc[:, :], sacc[:, :], tmp[sl][:, :], ALU.add)
                    ins.then_inc(sq_free.sem, 1)
                    at.step(sq_free)
                    return ins

                def sums(n):
                    for k in range(n):
                        accumulate(k)
                    finish_sums()

                def finish_sums():
                    dve.drain()
                    dve.memset(stat[:, 24:25], 0.0).then_inc(sum_full.sem, 1)
                    at.step(sum_full)

                def inverse():
                    at.step(root_full, NG)
                    dve.wait_ge(root_full.sem, at.value(root_full))
                    dve.reciprocal(rinv[:, :], rinv[:, :]).then_inc(r_full.sem, 1)
                    at.step(r_full)
                    dve.drain()

                def new_h(gain):
                    for k in range(KD):
                        at.step(hh_new)
                        dve.wait_ge(hh_new.sem, at.value(hh_new))
                        dve.scalar_tensor_tensor(out=hl[:, k, :], in0=x[:, k, :], scalar=gn[:, gain + k:gain + k + 1],
                                                 in1=hh[:, k, :].bitcast(F32), op0=ALU.mult,
                                                 op1=ALU.subtract).then_inc(hl_new.sem, 1)
                        at.step(hl_new)
                        accumulate(k)
                    finish_sums()
                    inverse()

                def new_x(xin, gain):
                    inverse()
                    at.step(x_loaded, 16)
                    dve.wait_ge(x_loaded.sem, at.value(x_loaded))
                    for k in range(KD):
                        dve.tensor_tensor(z[:, k, :], z[:, k, :], rinv[:, :], ALU.mult)
                        dve.drain()
                        dve.scalar_tensor_tensor(out=x[:, k, :], in0=z[:, k, :], scalar=gn[:, gain + k:gain + k + 1],
                                                 in1=xin[:, k, :], op0=ALU.mult, op1=ALU.add).then_inc(x_new.sem, 1)
                        at.step(x_new)

                at.step(small_in, 16)
                dve.wait_ge(small_in.sem, at.value(small_in))
                new_h(G_MIX_PRE)
                with dve.Fori(0, UNITS_IN // 2) as i:
                    at.enter(i, {acc_full: 2, acc_free: 2})
                    for s in range(2):
                        at.step(acc_full)
                        dve.wait_ge(acc_full.sem, at.value(acc_full))
                        for g in range(NG):
                            ins = dve.tensor_tensor(z[:, bass.ds(i * 2 + s, 1), cols(g)],
                                                    bank3(s, g).rearrange("p (a n) -> p a n", a=1),
                                                    rinv[:, cols(g)].rearrange("p (a n) -> p a n", a=1), ALU.mult)
                        ins.then_inc(acc_free.sem, 1)
                        at.step(acc_free)
                    at.leave(UNITS_IN // 2)
                dve.drain()
                dve.memset(stat[:, 25:26], 0.0).then_inc(z_done.sem, 1)
                at.step(z_done)
                for n, (first, w, gain) in enumerate(((Z_Q, 2, G_Q), (Z_C, 1, G_C), (Z_V, 4, G_V))):
                    sums(w)
                    inverse()
                    for k in range(w):
                        ins = dve.scalar_tensor_tensor(out=z[:, first + k, :], in0=z[:, first + k, :],
                                                       scalar=gn[:, gain + k:gain + k + 1], in1=rinv[:, :],
                                                       op0=ALU.mult, op1=ALU.mult)
                    ins.then_inc(zn_done.sem, 1)
                    at.step(zn_done)
                dve.drain()
                dve.tensor_tensor(t0[0:32, :], z[0:32, Z_K, :], trig[0:32, :], ALU.mult)
                dve.tensor_tensor(t1[0:32, :], z[32:64, Z_K, :], trig[32:64, :], ALU.mult)
                dve.drain()
                dve.tensor_tensor(z[0:32, Z_K, :], t0[0:32, :], t1[0:32, :], ALU.add).then_inc(zn_done.sem, 1)
                at.step(zn_done)
                dve.drain()
                at.step(x_stored, 16)
                dve.wait_ge(x_stored.sem, at.value(x_stored))
                dve.memset(wd, 0.0).then_inc(wd_zero.sem, 1)
                at.step(wd_zero)
                at.step(gate_in, gate_in.per)
                dve.wait_ge(gate_in.sem, at.value(gate_in))
                for g in range(GROUPS):
                    dve.tensor_tensor(ws[:, g, :], ws[:, g, :], tril, ALU.mult)
                for g in range(GROUPS):
                    ins = dve.tensor_tensor(wd[:, g, :], wd[:, g, :], cst[0:NS, C_WD:C_WD + NS], ALU.mult)
                dve.drain()
                dve.memset(stat[:, 25:26], 0.0).then_inc(ws_ready.sem, 1)
                at.step(ws_ready)
                for t in range(NB + 1):
                    at.step(mix_full)
                    dve.wait_ge(mix_full.sem, at.value(mix_full))
                    w = P if t < NB else NS
                    for a in range(2):
                        rows = slice(64 * a, 64 * a + 64)
                        for c in range(2):
                            src = ps[2 * (t % 2) + c][rows, 0:4 * w].rearrange("p (a e i) -> p a e i", a=2, e=2)[:, :, a, :]
                            dst = gt[rows, 2 * c:2 * c + 2, 0:w]
                            if t < NB:
                                dve.tensor_tensor(dst, src, bb[rows, 2 * c:2 * c + 2, :], ALU.add)
                            else:
                                for b in range(DB):
                                    dve.tensor_tensor(dst[:, :, DT * b:DT * b + DT], src[:, :, DT * b:DT * b + DT],
                                                      bb[rows, 2 * c:2 * c + 2, 0:DT], ALU.add)
                    dve.drain()
                    uu = z[:, Z_U:Z_U + 4, t * P:t * P + w]
                    dve.tensor_tensor(uu, uu, gt[:, :, 0:w], ALU.mult).then_inc(mix_free.sem, 1)
                    at.step(mix_free)
                    dve.drain()
                at.step(gateh)
                dve.wait_ge(gateh.sem, at.value(gateh))
                dve.tensor_tensor(hl[:, 4:8, :], z[:, Z_U:Z_U + 4, :], hh[:, 4:8, :].bitcast(F32),
                                  ALU.subtract).then_inc(gate_done.sem, 1)
                at.step(gate_done)
                at.step(outs, 80)
                dve.drain()
                dve.wait_ge(outs.sem, at.value(outs))
                dve.memset(qd, 0.0)
                dve.memset(qrd, 0.0)
                dve.drain()
                dve.memset(stat[:, 25:26], 0.0).then_inc(qd_zero.sem, 1)
                at.step(qd_zero)

                def head(hp, e):
                    for g in range(NG):
                        at.step(q_full)
                        dve.wait_ge(q_full.sem, at.value(q_full))
                        a, b = rt[0:32, 0:GW], rt[0:32, GW:2 * GW]
                        dve.tensor_tensor(a, ps[g][64:96, 0:GW], trig[64:96, cols(g)], ALU.mult)
                        dve.tensor_tensor(b, ps[g][96:128, 0:GW], trig[96:128, cols(g)], ALU.mult)
                        dve.drain()
                        dve.tensor_tensor(qp[0:32, cols(g)], a, b, ALU.add).then_inc(qp_new.sem, 1)
                        at.step(qp_new)
                        dve.drain()
                    src = qp[0:32, SEQ:TOK].rearrange("p (q b t) -> p q b t", q=QUADS, b=QB)
                    for q in range(QUADS):
                        dve.tensor_copy(qr[:, q, :, bass.ds(hp * 8 + 4 * e, 4)], src[:, q])
                    for j in range(NB):
                        at.step(s_full)
                        dve.wait_ge(s_full.sem, at.value(s_full))
                        c, w = j // 4, (j % 4) * P
                        bank = 2 * (j % 2)
                        dve.tensor_tensor(ps[bank + c][:, w:w + P], ps[bank + c][:, w:w + P], tri, ALU.add)
                        dve.drain()
                        st = 16 + 2 * (j % 2)
                        if c == 0:
                            dve.tensor_reduce(stat[:, st:st + 1], ps[bank][:, 0:w + P], AX.X, ALU.max)
                        else:
                            dve.tensor_reduce(stat[:, st:st + 1], ps[bank][:, :], AX.X, ALU.max)
                            dve.tensor_reduce(stat[:, st + 1:st + 2], ps[bank + 1][:, 0:w + P], AX.X, ALU.max)
                            dve.drain()
                            dve.tensor_tensor(stat[:, st:st + 1], stat[:, st:st + 1], stat[:, st + 1:st + 2], ALU.max)
                        dve.drain()
                        dve.tensor_scalar(stat[:, j % 2:j % 2 + 1], stat[:, st:st + 1], -SCALE, None,
                                          ALU.mult).then_inc(nmax.sem, 1)
                        at.step(nmax)
                        if j > 0:
                            normalise(j - 1)
                    normalise(NB - 1)

                def normalise(j):
                    at.step(exped)
                    dve.wait_ge(exped.sem, at.value(exped))
                    s = 2 + 2 * (j % 2)
                    if j >= 4:
                        dve.tensor_tensor(stat[:, s:s + 1], stat[:, s:s + 1], stat[:, s + 1:s + 2], ALU.add)
                        dve.drain()
                    dve.reciprocal(stat[:, 20 + j % 2:21 + j % 2], stat[:, s:s + 1])
                    dve.drain()
                    w = (j + 1) * P
                    dve.tensor_scalar(pr[:, j % 2, 0:w], pr[:, j % 2, 0:w], stat[:, 20 + j % 2:21 + j % 2], None,
                                      ALU.mult).then_inc(p_new.sem, 1)
                    at.step(p_new)

                with dve.Fori(0, HEADS // 2) as hp:
                    at.enter(hp, {q_full: 6, qp_new: 6, s_full: 16, nmax: 16, exped: 16, p_new: 16, abs_full: 6})
                    for e in range(2):
                        head(hp, e)
                        at.step(abs_full, 3)
                    at.leave(HEADS // 2)
                dve.drain()
                for b in range(QB):
                    for q in range(QUADS):
                        ins = dve.tensor_copy(qrd[32 * b:32 * b + 32, q, 32 * b:32 * b + 32], qr[:, q, b, :])
                for b in range(QB):
                    ins = dve.tensor_copy(kn[32 * b:32 * b + 32, :], z[0:32, Z_K, SEQ:TOK])
                dve.drain()
                at.step(o_new, 2 * HEADS)
                dve.wait_ge(o_new.sem, at.value(o_new))
                dve.memset(stat[:, 25:26], 0.0).then_inc(qrd_new.sem, 1)
                at.step(qrd_new)
                dve.memset(wv, 0.0).then_inc(wv_zero.sem, 1)
                at.step(wv_zero)

                def d_max(first=False, quad=0):
                    at.step(ds_full)
                    dve.wait_ge(ds_full.sem, at.value(ds_full))
                    s = d_max.n % 2
                    d_max.n += 1
                    if first:
                        dve.tensor_tensor(ps[5][:, 0:NS], ps[5][:, 0:NS],
                                          cst[:, C_NEW + NS * quad:C_NEW + NS * quad + NS], ALU.add)
                        dve.drain()
                        dve.tensor_reduce(stat[:, 8 + s:9 + s], ps[5][:, 0:NS], AX.X, ALU.max)
                    else:
                        dve.tensor_reduce(stat[:, 22:23], ps[5][:, :], AX.X, ALU.max)
                        dve.drain()
                        dve.tensor_tensor(stat[:, 8 + s:9 + s], stat[:, 22:23], stat[:, 8 + 1 - s:9 + 1 - s], ALU.max)
                    dve.drain()
                    dve.tensor_scalar(stat[:, 10 + s:11 + s], stat[:, 8 + s:9 + s], -SCALE, None,
                                      ALU.mult).then_inc(dmax.sem, 1)
                    at.step(dmax)

                def d_keys(s):
                    at.step(cache_in[s], 16 * 32)
                    dve.wait_ge(cache_in[s].sem, at.value(cache_in[s]))
                    dve.tensor_copy(rk2, rk[:, s, :, :, :].rearrange("p b r c -> p r b c")).then_inc(rk_new.sem, 1)
                    at.step(rk_new)
                    for b in (0, 1, 4):
                        at.step(dct_full, 5 if b == 0 else 0)
                        dve.wait_ge(dct_full.sem, at.value(dct_full, b - 4))
                        dve.tensor_copy(ctt[b] if b < 4 else rtt, ps[b][:, :]).then_inc(dct_dve.sem, 1)
                        at.step(dct_dve)

                def d_sum():
                    at.step(dexp)
                    dve.wait_ge(dexp.sem, at.value(dexp))
                    s = d_sum.n % 2
                    d_sum.n += 1
                    dve.scalar_tensor_tensor(out=stat[:, 23:24], in0=stat[:, 23:24], scalar=stat[:, 12 + s:13 + s],
                                             in1=stat[:, 14 + s:15 + s], op0=ALU.mult, op1=ALU.add)
                    dve.tensor_copy(stat[:, 4 + 2 + s:4 + 3 + s], stat[:, 12 + s:13 + s])
                    dve.drain()

                def d_out():
                    at.step(do_full)
                    dve.wait_ge(do_full.sem, at.value(do_full))
                    s = d_out.n % 2
                    d_out.n += 1
                    for b in range(QB):
                        r = slice(32 * b, 32 * b + 32)
                        ins = dve.scalar_tensor_tensor(out=oacc[r, :], in0=oacc[r, :], scalar=stat[r, 6 + s:7 + s],
                                                       in1=ps[7][r, P * b:P * b + P], op0=ALU.mult, op1=ALU.add)
                    ins.then_inc(do_free.sem, 1)
                    at.step(do_free)
                    dve.drain()

                for quad in range(QUADS):
                    d_max.n = 0
                    d_sum.n = d_out.n = 1
                    d_max(True, quad)
                    at.step(dexp)
                    dve.wait_ge(dexp.sem, at.value(dexp))
                    dve.tensor_copy(stat[:, 23:24], stat[:, 14:15])
                    dve.drain()
                    at.step(do_full)
                    dve.wait_ge(do_full.sem, at.value(do_full))
                    dve.tensor_copy(oacc, ps[7][:, 0:P]).then_inc(do_free.sem, 1)
                    at.step(do_free)
                    dve.drain()
                    d_keys(0)
                    d_max()
                    d_sum()
                    with dve.Fori(0, CHUNKS // 2 - 1) as i:
                        at.enter(i, {cache_in[0]: 512, cache_in[1]: 512, rk_new: 2, dct_full: 10, dct_dve: 6, ds_full: 2, dmax: 2, dexp: 2, do_full: 2, do_free: 2})
                        for s in range(2):
                            d_keys(1 - s)
                            d_max()
                            d_out()
                            d_sum()
                        at.leave(CHUNKS // 2 - 1)
                    d_keys(1)
                    d_max()
                    d_out()
                    d_sum()
                    d_out()
                    dve.reciprocal(stat[:, 22:23], stat[:, 23:24])
                    dve.drain()
                    dve.tensor_scalar(oacc, oacc, stat[:, 22:23], None, ALU.mult).then_inc(on_new.sem, 1)
                    at.step(on_new)
                    at.step(ot_full)
                    dve.wait_ge(ot_full.sem, at.value(ot_full))

                for u in range(UNITS_UV):
                    at.step(ab_h)
                    dve.wait_ge(ab_h.sem, at.value(ab_h))
                    for g in range(NG):
                        ins = dve.tensor_tensor(hl[:, u, cols(g)], bank3(u, g), hh[:, u, cols(g)].bitcast(F32),
                                                ALU.subtract)
                    ins.then_inc(acc_free.sem, 1)
                    at.step(acc_free)
                    at.step(acc_full)
                    dve.drain()
                    dve.memset(stat[:, 25:26], 0.0).then_inc(ab_l.sem, 1)
                    at.step(ab_l)
                sums(UNITS_OUT)
                at.step(acc_full, UNITS_OUT)
                at.step(acc_free, UNITS_OUT)
                new_x(x, G_MIX_POST)
                new_h(G_FFN_PRE)
                at.step(y_new, UNITS_OUT)
                dve.memset(z[:, 0:KD, :], 0.0)
                with dve.Fori(0, FB) as i:
                    at.enter(i, {acc_full: 12, acc_free: 12, act_new: 4, hid_h: 4, hid_l: 4})

                    def low(j):
                        at.step(hid_h)
                        dve.wait_ge(hid_h.sem, at.value(hid_h))
                        dve.tensor_tensor(hidl[:, j, :], z[:, 10 + j % 2, :], hidh[:, j, :].bitcast(F32),
                                          ALU.subtract).then_inc(hid_l.sem, 1)
                        at.step(hid_l)

                    for j in range(4):
                        at.step(acc_full)
                        dve.wait_ge(acc_full.sem, at.value(acc_full))
                        for g in range(NG):
                            ins = dve.scalar_tensor_tensor(out=z[:, 8 + j % 2, cols(g)], in0=bank3(j, g), scalar=0.0,
                                                           in1=rinv[:, cols(g)], op0=ALU.max, op1=ALU.mult)
                        ins.then_inc(acc_free.sem, 1)
                        at.step(acc_free)
                        dve.drain()
                        dve.memset(stat[:, 25:26], 0.0).then_inc(act_new.sem, 1)
                        at.step(act_new)
                        if j > 0:
                            low(j - 1)
                    low(3)
                    for m in range(UNITS_DOWN):
                        at.step(acc_full)
                        dve.wait_ge(acc_full.sem, at.value(acc_full))
                        for g in range(NG):
                            ins = dve.tensor_tensor(z[:, m, cols(g)], bank3(m, g), z[:, m, cols(g)], ALU.add)
                        ins.then_inc(acc_free.sem, 1)
                        at.step(acc_free)
                    dve.drain()
                    at.leave(FB)
                dve.drain()
                dve.memset(stat[:, 25:26], 0.0).then_inc(y_new.sem, 1 + UNITS_OUT)
                at.step(y_new)
                sums(KD)
                new_x(x2, G_FFN_POST)
                at.done()

        @block.tensor
        def _(pe):
            pe.wait_ge(s_first, 48)
            pe.wait_ge(s_init, 2)
            with pe.Fori(0, DEPTH) as l:
                at = Pos(l)

                def take_tile():
                    at.step(split)
                    pe.wait_ge(split.sem, at.value(split))

                held = [False]

                def release(ins):
                    if held[0]:
                        ins.then_inc(wfree.sem, 1)
                        at.step(wfree)
                        held[0] = False

                def release_now():
                    pe.wait_ge(acc_full.sem, at.value(acc_full))
                    pe.sem_inc(wfree.sem, 1)
                    at.step(wfree)
                    held[0] = False

                def dense(s, w0, kk, mh, ml, u, last_of_tile, ready=None):
                    at.step(acc_free)
                    pe.wait_ge(acc_free.sem, at.value(acc_free, -1))
                    for k in range(kk):
                        if ready is not None:
                            ready(k)
                        o = w0(k)
                        for n, (w, m) in enumerate(((wh, mh), (wh, ml), (wl, mh))):
                            for g in range(NG):
                                ins = pe.matmul(bank3(u, g), w[:, s, o:o + P], m[:, k, cols(g)],
                                                start=(k == 0 and n == 0), stop=(k == kk - 1 and n == 2))
                                release(ins)
                    ins.then_inc(acc_full.sem, 1)
                    at.step(acc_full)
                    held[0] = last_of_tile

                def means():
                    at.step(sum_full)
                    pe.wait_ge(sum_full.sem, at.value(sum_full))
                    for g in range(NG):
                        if g == 2:
                            pe.wait_ge(root_full.sem, at.value(root_full, 1))
                        pe.matmul(ps[6 + g % 2][:, 0:GW], ones[:, :], sacc[:, cols(g)],
                                  start=True, stop=True).then_inc(mean_full.sem, 1)
                        at.step(mean_full)
                    at.step(root_full, NG)

                def hl_ready(k):
                    at.step(hl_new)
                    pe.wait_ge(hl_new.sem, at.value(hl_new))

                take_tile()
                dense(0, lambda k: k * P, KD, hh, hl, 0, True, hl_ready)
                means()
                take_tile()
                dense(1, lambda k: k * P, KD, hh, hl, 1, True)
                with pe.Fori(1, UNITS_IN // 2) as i:
                    at.enter(i - 1, {split: 2, wfree: 2, acc_free: 2, acc_full: 2})
                    for s in range(2):
                        take_tile()
                        dense(s, lambda k: k * P, KD, hh, hl, s, True)
                    at.leave(UNITS_IN // 2 - 1)
                release_now()
                for n in range(3):
                    means()
                at.step(zn_done, 4)
                pe.wait_ge(zn_done.sem, at.value(zn_done))
                for t in range(NB + 1):
                    m = P if t < NB else NS
                    if t >= 2:
                        pe.wait_ge(ct_free.sem, at.value(ct_free, t - 1))
                    tk = slice(t * P, t * P + m)
                    pe.transpose(ps[4 + t % 2][0:m, 0:CL], z[:, Z_C, tk], ident)
                    pe.transpose(ps[4 + t % 2][0:m, CL:CL + ROPE], z[0:ROPE, Z_K, tk],
                                 ident[0:ROPE, 0:ROPE]).then_inc(ct_full.sem, 1)
                    at.step(ct_full)
                at.step(ct_free, NB + 1)

                def turn_v(t):
                    m = P if t < NB else NS
                    if t >= 2:
                        pe.wait_ge(vt_free.sem, at.value(vt_free, t - 1))
                    for i in range(4):
                        ins = pe.transpose(ps[6 + t % 2][0:m, i * P:(i + 1) * P], z[:, Z_V + i, t * P:t * P + m], ident)
                    ins.then_inc(vt_full.sem, 1)
                    at.step(vt_full)

                def mix(t):
                    pe.wait_ge(vt_free.sem, at.value(vt_free, t + 1))
                    if t >= 2:
                        pe.wait_ge(mix_free.sem, at.value(mix_free, t - 1))
                    m = P if t < NB else NS
                    w = ws if t < NB else wd
                    for a in range(4):
                        ins = pe.matmul(ps[2 * (t % 2) + a // 2][:, (a % 2) * 2 * m:(a % 2) * 2 * m + 2 * m],
                                        vn[0:m, t % 2, a * P:(a + 1) * P], w[:, 2 * a:2 * a + 2, :],
                                        start=True, stop=True)
                    ins.then_inc(mix_full.sem, 1)
                    at.step(mix_full)

                turn_v(0)
                at.step(ws_ready)
                pe.wait_ge(ws_ready.sem, at.value(ws_ready))
                for t in range(NB + 1):
                    if t < NB:
                        turn_v(t + 1)
                    mix(t)
                at.step(vt_free, NB + 1)
                at.step(mix_free, NB + 1)

                def scores(j):
                    n = (j + 1) * P
                    for c in range((n + 511) // 512):
                        w = min(512, n - 512 * c)
                        bank = ps[2 * (j % 2) + c][:, 0:w]
                        pe.matmul(bank, qa[:, j * P:(j + 1) * P], z[:, Z_C, 512 * c:512 * c + w], start=True, stop=False)
                        ins = pe.matmul(bank, qp[0:ROPE, j * P:(j + 1) * P], z[0:ROPE, Z_K, 512 * c:512 * c + w],
                                        start=False, stop=True)
                    ins.then_inc(s_full.sem, 1)
                    at.step(s_full)

                def turn_p(j):
                    at.step(p_new)
                    pe.wait_ge(p_new.sem, at.value(p_new))
                    for n in range(1 if j < 4 else 2):
                        bank = 4 + at.k.get(pt_full, 0) % 2
                        if at.k.get(pt_full, 0) - turn_p.first >= 2:
                            pe.wait_ge(pt_new.sem, at.value(pt_new, at.k[pt_full] - at.k.get(pt_new, 0) - 1))
                        for kb in range(4 * n, min(j + 1, 4 * n + 4)):
                            ins = pe.transpose(ps[bank][:, (kb % 4) * P:(kb % 4 + 1) * P],
                                               pr[:, j % 2, kb * P:(kb + 1) * P], ident)
                        ins.then_inc(pt_full.sem, 1)
                        at.step(pt_full)

                def values(sb_):
                    at.step(pt_new, 4 if sb_ == 0 else 8)
                    pe.wait_ge(pt_new.sem, at.value(pt_new))
                    if sb_ == 1:
                        pe.wait_ge(o_new.sem, at.value(o_new, 1))
                    nk = 4 * sb_ + 4
                    for kb in range(nk):
                        q0 = max(0, kb - 4 * sb_) * P
                        ins = pe.matmul(ps[6][:, q0:512], cn[:, kb, 0:CL], pt[:, kb, q0:512],
                                        start=(kb == 0), stop=(kb == nk - 1))
                    ins.then_inc(o_full.sem, 1)
                    at.step(o_full)

                def head(hp, e):
                    for g in range(NG):
                        for k in range(2):
                            ins = pe.matmul(ps[g][:, 0:GW], wq[:, e, k, :], z[:, Z_Q + k, cols(g)],
                                            start=(k == 0), stop=(k == 1))
                        ins.then_inc(q_full.sem, 1)
                        at.step(q_full)
                    for g in range(NG):
                        at.step(qn_new)
                        pe.wait_ge(qn_new.sem, at.value(qn_new))
                        pe.matmul(ps[3 + g][:, 0:GW], wk[:, e, :], qn[0:NOPE, cols(g)],
                                  start=True, stop=True).then_inc(abs_full.sem, 1)
                        at.step(abs_full)
                    at.step(qa_new, NG)
                    pe.wait_ge(qa_new.sem, at.value(qa_new))
                    at.step(qp_new, NG)
                    pe.wait_ge(qp_new.sem, at.value(qp_new))
                    turn_p.first = at.k.get(pt_full, 0)
                    scores(0)
                    for j in range(NB):
                        if j + 1 < NB:
                            if j >= 1:
                                pe.wait_ge(exped.sem, at.value(exped, j))
                            scores(j + 1)
                        turn_p(j)
                        if j == 3:
                            values(0)
                    values(1)
                    at.step(exped, NB)
                    at.step(o_new, 2)
                    pe.wait_ge(o_new.sem, at.value(o_new))

                with pe.Fori(0, HEADS // 2) as hp:
                    at.enter(hp, {wqk_in: 32, q_full: 6, qn_new: 6, qp_new: 6, abs_full: 6, qa_new: 6, s_full: 16,
                                  exped: 16, p_new: 16, pt_full: 24, pt_new: 24, o_full: 4, o_new: 4})
                    at.step(wqk_in, 32)
                    pe.wait_ge(mix_free.sem, at.value(mix_free))
                    pe.wait_ge(wqk_in.sem, at.value(wqk_in))
                    for e in range(2):
                        head(hp, e)
                    at.leave(HEADS // 2)

                at.step(qrd_new)
                pe.wait_ge(qrd_new.sem, at.value(qrd_new))

                def q_of(quad, b):
                    return qd[:, quad, b * P:(b + 1) * P]

                def d_turn(s):
                    at.step(cache_in[s], 16 * 32)
                    pe.wait_ge(cache_in[s].sem, at.value(cache_in[s]))
                    for b in range(QB + 1):
                        if at.k.get(dct_full, 0) > 4:
                            if b in (2, 3):
                                pe.wait_ge(dct_act.sem, at.value(dct_act, b - 3))
                            else:
                                pe.wait_ge(dct_dve.sem, at.value(dct_dve, {0: -2, 1: -1, 4: 0}[b]))
                        if b == QB:
                            at.step(rk_new)
                            pe.wait_ge(rk_new.sem, at.value(rk_new))
                        for r in range(4):
                            src = ck[:, s, b, r, :] if b < QB else rk2[:, r, :, :].rearrange("p b c -> p (b c)")
                            ins = pe.transpose(ps[b][:, r * P:(r + 1) * P], src, ident)
                        ins.then_inc(dct_full.sem, 1)
                        at.step(dct_full)
                    at.step(dct_act, 2)
                    at.step(dct_dve, 3)

                def d_scores(quad):
                    pe.wait_ge(dexp.sem, at.value(dexp))
                    pe.wait_ge(dct_act.sem, at.value(dct_act))
                    pe.wait_ge(dct_dve.sem, at.value(dct_dve))
                    for b in range(QB):
                        pe.matmul(ps[5][:, :], q_of(quad, b), ctt[b], start=(b == 0), stop=False)
                    pe.matmul(ps[5][:, :], qrd[:, quad, :], rtt, start=False, stop=True).then_inc(ds_full.sem, 1)
                    at.step(ds_full)

                def d_turn_p():
                    at.step(dexp)
                    pe.wait_ge(dexp.sem, at.value(dexp))
                    for r in range(4):
                        ins = pe.transpose(ps[6][:, r * P:(r + 1) * P], pd[:, r * P:(r + 1) * P], ident)
                    ins.then_inc(dpt_full.sem, 1)
                    at.step(dpt_full)

                def d_values(s):
                    at.step(dpt_new)
                    pe.wait_ge(dpt_new.sem, at.value(dpt_new))
                    pe.wait_ge(do_free.sem, at.value(do_free))
                    at.step(do_free)
                    for r in range(4):
                        ins = pe.matmul(ps[7][:, :], ptd[:, r, :], ck[:, s, :, r, :], start=(r == 0), stop=(r == 3))
                    ins.then_inc(do_full.sem, 1)
                    at.step(do_full)
                    pe.wait_ge(do_full.sem, at.value(do_full))
                    pe.sem_inc(cache_free.sem, 1)
                    at.step(cache_free)

                for quad in range(QUADS):
                    if quad:
                        pe.wait_ge(dexp.sem, at.value(dexp))
                    for b in range(QB):
                        pe.matmul(ps[5][:, 0:NS], q_of(quad, b), z[:, Z_C, SEQ:TOK], start=(b == 0), stop=False)
                    pe.matmul(ps[5][:, 0:NS], qrd[:, quad, :], kn, start=False, stop=True).then_inc(ds_full.sem, 1)
                    at.step(ds_full)
                    at.step(dexp)
                    pe.wait_ge(dexp.sem, at.value(dexp))
                    if quad:
                        pe.wait_ge(ol_new.sem, at.value(ol_new))
                        pe.wait_ge(do_free.sem, at.value(do_free))
                    pe.transpose(ps[6][0:NS, 0:P], pd[:, 0:NS], ident).then_inc(dpt_full.sem, 1)
                    at.step(dpt_full)
                    at.step(dpt_new)
                    pe.wait_ge(dpt_new.sem, at.value(dpt_new))
                    pe.matmul(ps[7][:, 0:P], ptd[0:NS, 0, :], cn[0:NS, NB, 0:CL], start=True,
                              stop=True).then_inc(do_full.sem, 1)
                    at.step(do_full)
                    at.step(do_free)
                    d_turn(0)
                    d_scores(quad)
                    with pe.Fori(0, CHUNKS // 2 - 1) as i:
                        at.enter(i, {cache_in[0]: 512, cache_in[1]: 512, rk_new: 2, cache_free: 2, dct_full: 10, dct_act: 4,
                                     dct_dve: 6, dexp: 2, ds_full: 2, dpt_full: 2, dpt_new: 2, do_full: 2, do_free: 2})
                        for s in range(2):
                            d_turn(1 - s)
                            d_turn_p()
                            d_scores(quad)
                            d_values(s)
                        at.leave(CHUNKS // 2 - 1)
                    d_turn(1)
                    d_turn_p()
                    d_scores(quad)
                    d_values(0)
                    d_turn_p()
                    d_values(1)
                    at.step(on_new)
                    pe.wait_ge(on_new.sem, at.value(on_new))
                    pe.transpose(ps[6][:, 0:P], oacc, ident).then_inc(ot_full.sem, 1)
                    at.step(ot_full)
                    at.step(ol_new)
                pe.wait_ge(ol_new.sem, at.value(ol_new))
                at.step(wv_in, 32)
                pe.wait_ge(wv_in.sem, at.value(wv_in))
                for u in range(UNITS_UV):
                    at.step(acc_free)
                    pe.wait_ge(acc_free.sem, at.value(acc_free, -1))
                    for e in range(2):
                        for g in range(NG):
                            ins = pe.matmul(bank3(u, g), wv[:, 2 * u + e, :], z[:, Z_U + 2 * u + e, cols(g)],
                                            start=(e == 0), stop=(e == 1))
                    ins.then_inc(acc_full.sem, 1)
                    at.step(acc_full)
                at.step(ab_l, UNITS_UV)
                pe.wait_ge(ab_l.sem, at.value(ab_l))
                for u in range(2):
                    take_tile()
                    dense(u, lambda k: k * P, KD, hh, hl, u, True)
                with pe.Fori(1, UNITS_OUT // 2) as i:
                    at.enter(i - 1, {split: 2, wfree: 2, acc_free: 2, acc_full: 2})
                    for s in range(2):
                        take_tile()
                        dense(s, lambda k: k * P, KD, hh, hl, s, True)
                    at.leave(UNITS_OUT // 2 - 1)
                release_now()
                means()
                def up(j, ready=None):
                    take_tile()
                    dense(j % 2, lambda k: k * P, KD, hh, hl, j, True, ready)

                def down(m, ready=None):
                    if m % 2 == 0:
                        take_tile()
                    dense((m // 2) % 2, lambda k: k * 2 * P + (m % 2) * P, 4, hidh, hidl, m, m % 2 == 1, ready)

                def hid_ready(k):
                    at.step(hid_l)
                    pe.wait_ge(hid_l.sem, at.value(hid_l))

                up(0, hl_ready)
                means()
                for j in range(1, 4):
                    up(j)
                for m in range(UNITS_DOWN):
                    down(m, hid_ready if m == 0 else None)
                with pe.Fori(1, FB) as i:
                    at.enter(i - 1, {split: 8, wfree: 8, acc_free: 12, acc_full: 12, hid_l: 4})
                    for j in range(4):
                        up(j)
                    for m in range(UNITS_DOWN):
                        down(m, hid_ready if m == 0 else None)
                    at.leave(FB - 1)
                release_now()
                means()
                at.done()


def _constants():
    pos = np.concatenate([np.arange(SEQ), np.tile(PAST + np.arange(DT), DB)]).astype(np.float32)
    half = ROPE // 2
    freqs = np.power(np.float32(10000.0), (-np.arange(half, dtype=np.float32) / np.float32(half))).astype(np.float32)
    ang = (pos[:, None] * freqs[None, :]).astype(np.float32)
    cos, sin = np.cos(ang).T, np.sin(ang).T
    c = np.zeros((P, C_ALL), np.float32)
    for base in (0, 64):
        c[base:base + 32, 0:TOK] = np.concatenate([cos, cos])
        c[base + 32:base + 64, 0:TOK] = np.concatenate([-sin, sin])
    i = np.arange(P)
    c[:, C_ID:C_ID + P] = np.eye(P)
    c[:, C_TRI:C_TRI + P] = np.where(i[None, :] <= i[:, None], 0.0, NEG)
    c[:, C_TRIL:C_TRIL + P] = i[None, :] >= i[:, None]
    j = np.arange(NS)
    for quad in range(QUADS):
        own = (j[None, :] // DT == quad * QB + i[:, None] // 32) & (j[None, :] % DT <= i[:, None] % DT)
        c[:, C_NEW + NS * quad:C_NEW + NS * quad + NS] = np.where(own, 0.0, NEG)
    c[0:NS, C_WD:C_WD + NS] = (j[:, None] // DT == j[None, :] // DT) & (j[:, None] % DT <= j[None, :] % DT)
    return c


def kernel(**inputs):
    import concourse.bacc as _bacc
    from concourse.bass_utils import run_bass_kernel_spmd as _run

    a = {k: np.asarray(v) for k, v in inputs.items()}
    x = np.concatenate([a["x_prompt"].reshape(SEQ, D), a["x_sample"].reshape(NS, D)])
    w = a["w_in"]
    s1, s2, s3, s4 = QL, QL + CL, QL + CL + ROPE, QL + CL + ROPE + GM
    half = ROPE // 2
    kpe = w[:, :, s2:s3]
    swp = np.concatenate([kpe[:, :, half:], kpe[:, :, :half]], axis=2)
    w = np.concatenate([w[:, :, :s2], kpe, swp, kpe, swp, w[:, :, s3:s4], w[:, :, s4:]], axis=2)

    def tiles(m, n):
        L, K, N = m.shape
        return m.reshape(L, K // P, P, N // n, n).transpose(0, 3, 2, 1, 4).reshape(L, N // n, P, -1)

    up = tiles(a["w_ff_up"], P).reshape(DEPTH, FB, 4, P, TW)
    dn = a["w_ff_down"].reshape(DEPTH * FB, FF // FB, D)
    dn = tiles(dn, 2 * P).reshape(DEPTH, FB, 4, P, TW)
    ff = np.concatenate([up, dn], axis=2).reshape(DEPTH, FB * 8, P, TW)
    stream = np.concatenate([tiles(w, P), tiles(a["w_out"], P), ff], axis=1)

    def col(g):
        return g.reshape(DEPTH, -1, P).transpose(0, 2, 1)

    gains = np.concatenate([col(a[n]) for n in ("norm_mix_pre", "norm_mix_post", "norm_ffn_pre", "norm_ffn_post",
                                                "q_norm", "kv_norm", "v_norm")], axis=2)
    q = a["w_uq"]
    qpe = q[..., NOPE:]
    q = np.concatenate([q, qpe[..., half:], qpe[..., :half]], axis=3)
    wuq = q.reshape(DEPTH, 2, P, HEADS // 2, 2, P).transpose(0, 3, 2, 4, 1, 5)
    wuk = a["w_uk"].transpose(0, 2, 3, 1).reshape(DEPTH, HEADS // 2, 2, NOPE, CL).transpose(0, 1, 3, 2, 4)
    wsp = a["w_spatial"].transpose(0, 3, 1, 2)
    bsp = np.repeat(a["b_spatial"].reshape(DEPTH, 4, 2, P).transpose(0, 2, 1, 3), 64, axis=1)
    arrays = {
        "xT": x.T.reshape(KD, P, TOK), "wst": stream, "gains": gains, "wuq": wuq, "wuk": wuk, "wuv": a["w_uv"],
        "wsp": wsp, "bsp": bsp,
        "cache_c": a["cache_kv_latent"].reshape(DEPTH * N_PHYS, 32, 4, CL),
        "cache_k": a["cache_k_rope"].reshape(DEPTH * N_PHYS, 32, 4, ROPE),
        "pages": a["page_table"].reshape(1, DB * PAGES), "consts": _constants(),
    }
    arrays = {k: np.ascontiguousarray(v) for k, v in arrays.items()}
    nc = _bacc.Bacc("TRN2", target_bir_lowering=False, num_devices=1)
    ins = [nc.dram_tensor(k, v.shape, mybir.dt.from_np(v.dtype), kind="ExternalInput").ap() for k, v in arrays.items()]
    shapes = {"yT": (KD, P, TOK), "o_cp": (DEPTH, NB, P, CL), "o_kp": (DEPTH, NB, P, ROPE), "o_cs": (DEPTH, NS, CL),
              "o_ks": (DEPTH, NS, ROPE), "o_vs": (DEPTH, NS, GM)}
    outs = [nc.dram_tensor(k, s, F32, kind="ExternalOutput").ap() for k, s in shapes.items()]
    spill = nc.dram_tensor("x_spill", (KD, P, TOK), F32, kind="Internal").ap()
    build(nc, *ins, *outs, spill)
    r = _run(nc, [arrays], core_ids=[0]).results[0]
    y = np.ascontiguousarray(r["yT"].reshape(D, TOK).T)
    return (y[:SEQ].reshape(1, SEQ, D), y[SEQ:].reshape(DB, DT, D),
            r["o_cp"].reshape(DEPTH, 1, NB, P, CL), r["o_kp"].reshape(DEPTH, 1, NB, P, ROPE),
            r["o_cs"].reshape(DEPTH, DB, DT, CL), r["o_ks"].reshape(DEPTH, DB, DT, ROPE),
            r["o_vs"].reshape(DEPTH, DB, DT, GM))
```

```python
from contextlib import ExitStack

import numpy as np

import concourse.bass as bass
from concourse import mybir

F32 = mybir.dt.float32
F32R = mybir.dt.float32r
I32 = mybir.dt.int32
ALU = mybir.AluOpType
ACT = mybir.ActivationFunctionType
AX = mybir.AxisListType

P = 128
D = 1024
KD = D // P
DEPTH = 2
SEQ = 1024
DB, DT = 8, 4
NS = DB * DT
TOK = SEQ + NS
NG, GW = 3, TOK // 3
NB = SEQ // P
HEADS, NOPE, ROPE, VD = 8, 64, 32, 64
QL, CL = 256, 128
GM = 512
GROUPS = 8
FF = 4096
FB = 8
PAST, PAGE = 4096, 128
PAGES = PAST // PAGE
N_PHYS = DB * PAGES * 5 // 4
SCALE = float((NOPE + ROPE) ** -0.5)
NEG = -1e30
EPS = 1e-6
TW = 1024

Z_Q, Z_C, Z_K, Z_V, Z_U, NZ = 0, 2, 3, 4, 8, 12
Z_O = Z_V
UNITS_IN, UNITS_UV, UNITS_OUT, UNITS_UP, UNITS_DOWN = NZ, 4, KD, 4, KD
TILES_LAYER = NZ + KD + FB * 8
UNITS_LAYER = UNITS_IN + UNITS_UV + UNITS_OUT + FB * (UNITS_UP + UNITS_DOWN)
G_MIX_PRE, G_MIX_POST, G_FFN_PRE, G_FFN_POST, G_Q, G_C, G_V, NGAIN = 0, 8, 16, 24, 32, 34, 35, 39
C_TRIG, C_ID, C_TRI, C_TRIL, C_NEW, C_WD = 0, TOK, TOK + P, TOK + 2 * P, TOK + 3 * P, TOK + 3 * P + 2 * NS
C_ROW = C_WD + NS
C_ALL = C_ROW + 1
Q_AT, ABS_AT = (2, 3, 4), (5, 6, 7)
QUADS, QB = DB // 4, 4
CHUNKS = PAST // 512
X_SP = 2


class Count:

    def __init__(self, sem, per_layer, credit=0):
        self.sem, self.per, self.credit = sem, per_layer, credit


class Pos:

    def __init__(self, layer, ahead={}):
        self.layer, self.k, self.base, self.ahead = layer, dict(ahead), [], ahead

    def value(self, s, more=0):
        v = self.layer * s.per + (s.credit + self.k.get(s, 0) + more)
        for i, steps in self.base:
            if s in steps:
                v = v + i * steps[s]
        return v

    def step(self, s, n=1):
        self.k[s] = self.k.get(s, 0) + n

    def enter(self, i, steps):
        self.base.append((i, steps))
        self.at = dict(self.k)

    def leave(self, trips):
        _, steps = self.base.pop()
        for s in set(self.k) | set(steps):
            got = self.k.get(s, 0) - self.at.get(s, 0)
            assert got == steps.get(s, 0), (s.sem, got, steps.get(s, 0))
            self.k[s] = self.at.get(s, 0) + trips * got

    def done(self):
        for s, n in self.k.items():
            assert n <= s.per + self.ahead.get(s, 0), (s.sem, n, s.per)


def build(nc, xT, wst, gains, pre, wuq, wuk, wuv, wsp, bsp, cache_c, cache_k, pages, consts,
          yT, o_cp, o_kp, o_cs, o_ks, o_vs, x_spill):
    with ExitStack() as ctx:
        def sb(name, shape, dt=F32):
            return ctx.enter_context(nc.sbuf_tensor(name, shape, dt))

        def sem(name):
            return ctx.enter_context(nc.semaphore(name))

        with nc.sbuf_tensor("x2", [P, KD, TOK], F32) as x2:
            pass
        with nc.sbuf_tensor("free_a", [P, 4 * TOK], F32) as free_a:
            pass
        hh = sb("hh", [P, KD, TOK], F32R)
        with nc.sbuf_tensor("free_b", [P, 4 * TOK], F32) as free_b:
            pass
        hl = sb("hl", [P, KD, TOK], F32R)
        with nc.sbuf_tensor("x", [P, KD, TOK], F32) as x:
            pass
        with nc.sbuf_tensor("scratch", [P, KD * TOK], F32) as scr:
            pass
        hidh = sb("hidh", [P, 4, TOK], F32R)
        hidl = sb("hidl", [P, 4, TOK], F32R)
        z = sb("z", [P, NZ, TOK])
        raw = sb("raw", [P, 2, TW])
        wh = sb("wh", [P, 2, TW], F32R)
        wl = sb("wl", [P, 2, TW], F32R)
        t0 = sb("t0", [P, TOK])
        t1 = sb("t1", [P, TOK])
        rinv = sb("rinv", [P, TOK])
        sacc = sb("sacc", [P, TOK])
        cst = sb("cst", [P, C_ALL])
        cn = sb("cn", [P, NB + 1, CL + ROPE])
        gn = sb("gn", [P, NGAIN])
        gpre = sb("gpre", [P, KD])
        ones = sb("ones", [P, P])
        eps = sb("eps", [P, 1])
        stat = sb("stat", [P, 64])
        marks = sb("marks", [P, QUADS * CHUNKS + 1])
        kpt = sb("kpt", [P, DB * CHUNKS], I32)
        crows = sb("crows", [P, DB * CHUNKS], I32)

        trig = cst[:, C_TRIG:C_TRIG + TOK]
        ident = cst[:, C_ID:C_ID + P]
        tri = cst[:, C_TRI:C_TRI + P]
        tril = cst[:, C_TRIL:C_TRIL + P]
        tmp = [t0, t1]

        rin2 = scr[:, 0:TOK]
        ws = scr[:, 1056:2080].rearrange("p (g i) -> p g i", g=GROUPS)
        bb = scr[:, 2080:2592].rearrange("p (a i) -> p a i", a=4)
        wd = scr[0:NS, 2592:2848].rearrange("p (g i) -> p g i", g=GROUPS)
        vn = scr[:, 2848:3872].rearrange("p (b n) -> p b n", b=2)
        gt = scr[:, 3872:4896].rearrange("p (b a i) -> p b a i", b=2, a=4)
        kr = scr[0:ROPE, 4896:4896 + 2 * TOK].rearrange("p (b n) -> p b n", b=2)
        qd = scr[:, 0:1280].rearrange("p (q n) -> p q n", q=QUADS)
        qrd = scr[:, 1280:1536].rearrange("p (q n) -> p q n", q=QUADS)
        qr = scr[0:ROPE, 1536:1792].rearrange("p (q b n) -> p q b n", q=QUADS, b=QB)
        pts = [scr[:, 5888:5888 + 2048].rearrange("p (k n) -> p k n", k=4),
               scr[:, 1792:1792 + 4096].rearrange("p (k n) -> p k n", k=NB)]
        wq = scr[:, 7936:8448].rearrange("p (h k n) -> p h k n", h=2, k=2)
        pr = free_a[:, 0:4096].rearrange("p (b n) -> p b n", b=4)
        qa = free_b[:, 0:2 * TOK].rearrange("p (e n) -> p e n", e=2)
        qp = free_b[0:ROPE, 2 * TOK:4 * TOK].rearrange("p (e n) -> p e n", e=2)
        cks = [f[:, 2048 * e:2048 * e + 2048].rearrange("p (b r c) -> p b r c", b=QB, r=4)
               for f in (free_a, free_b) for e in range(2)]
        rks = [scr[:, 1792 + 512 * e:2304 + 512 * e].rearrange("p (b r c) -> p b r c", b=QB, r=4) for e in range(4)]
        rk2 = scr[:, 7936:8448].rearrange("p (r b c) -> p r b c", r=4, b=QB)
        wv = scr[:, 6912:7936].rearrange("p (h n) -> p h n", h=HEADS)
        wk = sb("wk", [NOPE, 2, CL])
        qn, rt = t0, sacc
        ctt = [t0[:, 0:512], t0[:, 512:1024], t1[:, 0:512], t1[:, 512:1024]]
        rtt = sacc[:, 0:512]
        pd = rinv[:, 0:512]
        ptd = rinv[:, 512:1024].rearrange("p (r n) -> p r n", r=4)
        oacc = sacc[:, 512:640]
        kn = sacc[:, 640:672]

        psum = ctx.enter_context(nc.psum_tensor("psum", [P, 8, 512], F32))
        ps = [psum[:, i, :] for i in range(8)]

        S = {}

        def count(name, per, credit=0):
            S[name] = Count(sem(name), per, credit)
            return S[name]

        raw_in = [count(f"raw_in{i}", 16 * TILES_LAYER // 2) for i in range(2)]
        split = count("split", TILES_LAYER, 2)
        wfree = count("wfree", TILES_LAYER, 2)
        acc_full = count("acc_full", UNITS_LAYER)
        acc_free = count("acc_free", UNITS_LAYER, 2)
        x_new = count("x_new", 2 * KD, KD)
        hh_new = count("hh_new", 2 * KD)
        hl_new = count("hl_new", 2 * KD)
        SQ_TILES = 8 + 2 + 1 + 4 + 8 + 8 + 8
        sq_full = count("sq_full", SQ_TILES)
        sq_free = count("sq_free", SQ_TILES, 2)
        sum_full = count("sum_full", 7)
        mean_full = count("mean_full", 21)
        mean_read = count("mean_read", 21)
        root_full = count("root_full", 7)
        zn_done = count("zn_done", 4)
        x_stored = count("x_stored", 32)
        x_loaded = count("x_loaded", 32)
        s_first = sem("first_loads")
        s_x = [sem(f"x_first{k}") for k in range(KD)]
        pre_in = count("pre_in", 16, 16)
        small_in = count("small_in", 16)
        gate_in = count("gate_in", 16 * (2 + DB))
        wd_zero = count("wd_zero", 1)
        ws_ready = count("ws_ready", 1)
        ct_full = count("ct_full", NB + 1)
        ct_free = count("ct_free", NB + 1)
        vt_full = count("vt_full", NB + 1)
        vt_free = count("vt_free", NB + 1)
        mix_full = count("mix_full", NB + 1)
        mix_free = count("mix_free", NB + 1)
        gated = count("gated", NB + 1)
        gate_done = count("gate_done", 1)
        outs = count("outs", 16 * 5)
        qd_zero = count("qd_zero", 1)
        wqk_in = count("wqk_in", 16 * 2 * HEADS)
        q_full = count("q_full", 3 * HEADS)
        qn_new = count("qn_new", 3 * HEADS)
        qp_new = count("qp_new", 3 * HEADS)
        abs_full = count("abs_full", 3 * HEADS)
        qa_new = count("qa_new", 3 * HEADS, 1)
        s_full = count("s_full", NB * HEADS)
        nmax = count("nmax", NB * HEADS)
        exped = count("exped", NB * HEADS)
        p_new = count("p_new", NB * HEADS)
        pt_full = count("pt_full", 12 * HEADS)
        pt_new = count("pt_new", 12 * HEADS)
        o_full = count("o_full", 2 * HEADS)
        o_new = count("o_new", 2 * HEADS, 1)
        qrd_new = count("qrd_new", 1)
        n_step = QUADS * CHUNKS
        cache_in = [count(f"cache_in{i}", 16 * 2 * QB * n_step // 4) for i in range(4)]
        rk_new = count("rk_new", n_step)
        cache_free = count("cache_free", n_step)
        wv_zero = count("wv_zero", 1)
        wv_in = count("wv_in", 32)
        dct_full = count("dct_full", 5 * n_step)
        dct_act = count("dct_act", 2 * n_step)
        dct_dve = count("dct_dve", 3 * n_step)
        ds_full = count("ds_full", n_step + QUADS)
        dmax = count("dmax", n_step + QUADS)
        dexp = count("dexp", n_step + QUADS)
        dpt_full = count("dpt_full", n_step + QUADS)
        dpt_new = count("dpt_new", n_step + QUADS)
        do_full = count("do_full", n_step + QUADS)
        do_free = count("do_free", n_step + QUADS)
        kn_new = count("kn_new", 1)
        on_new = count("on_new", QUADS)
        ot_full = count("ot_full", QUADS)
        ol_new = count("ol_new", QUADS)
        ab_h = count("ab_h", UNITS_UV)
        ab_l = count("ab_l", UNITS_UV)
        y_new = count("y_new", KD)
        act_new = count("act_new", 4 * FB)
        hid_h = count("hid_h", 4 * FB)
        hid_l = count("hid_l", 4 * FB)
        s_init = sem("init")
        s_out = sem("written")

        block = ctx.enter_context(nc.Block())

        def groups(ap):
            return ap.rearrange("p (g n) -> p g n", g=NG)

        def s_of(j):
            first = 512 * j if j < 4 else 1024 * (j % 2)
            return psum[:, :, :].rearrange("p b n -> p (b n)")[:, first:first + (j + 1) * P]

        def bank3(u, g):
            return psum[:, 3 * (u % 2) + g, 0:GW]

        def acc(u):
            return psum[:, 3 * (u % 2):3 * (u % 2) + NG, 0:GW]

        def cols(g):
            return slice(g * GW, (g + 1) * GW)

        @block.sync
        def _(sp):
            sp.dma_start(gpre[:, :], pre[DEPTH - 1]).then_inc(pre_in.sem, 16)
            for k in range(X_SP):
                sp.dma_start(x[:, k, :], xT[k]).then_inc(s_x[k], 16)
            sp.dma_start(cst[:, :], consts).then_inc(s_first, 16)
            sp.dma_start(kpt[:, :], pages).then_inc(s_first, 16)
            with sp.Fori(0, DEPTH) as l:
                at = Pos(l)

                def tile_in(t):
                    sp.wait_ge(split.sem, at.value(split, -1))
                    at.step(split)
                    sl = raw_in[t % 2]
                    sp.dma_start(raw[:, t % 2, :], wst[l, t]).then_inc(sl.sem, 16)

                for t in range(4):
                    tile_in(t)
                sp.wait_ge(x_new.sem, at.value(x_new))
                sp.dma_start(gn[:, :], gains[l]).then_inc(small_in.sem, 16)
                sp.dma_start(x_spill.rearrange("k p t -> p k t"), x[:, :, :]).then_inc(x_stored.sem, 16)
                tile_in(4)
                at.step(x_stored, 16)
                sp.wait_ge(x_stored.sem, at.value(x_stored))
                at.step(hl_new, KD)
                sp.wait_ge(hl_new.sem, at.value(hl_new))
                sp.dma_start(ws, wsp[l]).then_inc(gate_in.sem, 16)
                sp.dma_start(bb, bsp[l]).then_inc(gate_in.sem, 16)
                at.step(wd_zero)
                sp.wait_ge(wd_zero.sem, at.value(wd_zero))
                for b in range(DB):
                    sp.dma_start(wd[DT * b:DT * b + DT, :, DT * b:DT * b + DT],
                                 wsp[l][0:DT, :, 0:DT]).then_inc(gate_in.sem, 16)
                for t in range(5, NZ):
                    tile_in(t)
                for t in range(NZ, NZ + 2):
                    tile_in(t)
                at.step(ct_free, NB + 1)
                sp.wait_ge(ct_free.sem, at.value(ct_free))
                sp.dma_start(o_cp[l].rearrange("n p c -> p n c"), cn[:, 0:NB, 0:CL]).then_inc(outs.sem, 16)
                sp.dma_start(o_kp[l].rearrange("n p c -> p n c"), cn[:, 0:NB, CL:]).then_inc(outs.sem, 16)
                sp.dma_start(o_cs[l], cn[0:NS, NB, 0:CL]).then_inc(outs.sem, 16)
                sp.dma_start(o_ks[l], cn[0:NS, NB, CL:]).then_inc(outs.sem, 16)
                at.step(vt_free, NB + 1)
                sp.wait_ge(vt_free.sem, at.value(vt_free))
                sp.dma_start(o_vs[l], vn[0:NS, NB % 2, :]).then_inc(outs.sem, 16)
                at.step(wv_zero)
                sp.wait_ge(wv_zero.sem, at.value(wv_zero))
                for e in range(2):
                    dst = wv.rearrange("p (a e) n -> p a e n", e=2)[:, :, e, VD * e:VD * e + VD]
                    src = wuv[l].rearrange("c (a e) v -> c a e v", e=2)[:, :, e, :]
                    sp.dma_start(dst, src).then_inc(wv_in.sem, 16)

                at.step(ab_l, UNITS_UV)
                sp.wait_ge(ab_l.sem, at.value(ab_l))
                sp.dma_start(x[:, :, :], x_spill.rearrange("k p t -> p k t")).then_inc(x_loaded.sem, 16)
                for t in range(NZ + 2, NZ + KD + 4):
                    tile_in(t)
                at.step(x_new, KD)
                sp.wait_ge(x_new.sem, at.value(x_new))
                sp.dma_start(x_spill.rearrange("k p t -> p k t"), x[:, :, :]).then_inc(x_stored.sem, 16)
                sp.dma_start(gpre[:, :], pre[l]).then_inc(pre_in.sem, 16)
                base = NZ + KD + 4
                with sp.Fori(0, FB - 1) as i:
                    at.enter(i, {split: 8})
                    for t in range(8):
                        sp.wait_ge(split.sem, at.value(split, -1))
                        at.step(split)
                        sp.dma_start(raw[:, t % 2, :], wst[l, i * 8 + (base + t)]).then_inc(raw_in[t % 2].sem, 16)
                    at.leave(FB - 1)
                for t in range(base + (FB - 1) * 8, TILES_LAYER):
                    tile_in(t)
                at.step(acc_full, UNITS_LAYER - KD)
                sp.wait_ge(acc_full.sem, at.value(acc_full))
                at.step(acc_full, KD)
                at.step(x_stored, 16)
                sp.dma_start(x2[:, :, :], x_spill.rearrange("k p t -> p k t")).then_inc(x_loaded.sem, 16)
                at.step(x_new, KD)
                at.step(hl_new, KD)
                at.done()
            for k in range(KD):
                sp.wait_ge(x_new.sem, DEPTH * x_new.per + k + 1)
                sp.dma_start(yT[k], x[:, k, :]).then_inc(s_out, 16)
            sp.wait_ge(s_out, 16 * KD)
            sp.wait_ge(outs.sem, DEPTH * outs.per)
            sp.wait_ge(x_stored.sem, DEPTH * x_stored.per)

        @block.gpsimd
        def _(pool):
            pool.memset(ones[:, :], 1.0).then_inc(s_init, 1)
            pool.memset(eps[:, :], EPS).then_inc(s_init, 1)
            pool.memset(stat[:, 30:31], 0.0).then_inc(split.sem, 2)
            pool.memset(stat[:, 31:32], 0.0).then_inc(wfree.sem, 2)

            def sums_x():
                for k in range(KD):
                    at.step(sq_full)
                    pool.drain()
                    pool.wait_ge(sq_full.sem, at.value(sq_full))
                    sl = (at.k[sq_full] - 1) % 2
                    if k == 0:
                        ins = pool.tensor_tensor(sacc[:, :], tmp[sl][:, :], ones[:, 0:1].to_broadcast([P, TOK]),
                                                 ALU.mult)
                    else:
                        ins = pool.tensor_tensor(sacc[:, :], sacc[:, :], tmp[sl][:, :], ALU.add)
                    ins.then_inc(sq_free.sem, 1)
                pool.drain()
                mark = marks[:, QUADS * CHUNKS:]
                pool.tensor_tensor(mark, ones[:, 0:1], ones[:, 0:1], ALU.mult).then_inc(sum_full.sem, 1)

            with pool.Fori(0, DEPTH) as l:
                at = Pos(l)

                def split_tiles(n):
                    with pool.Fori(0, n // 2) as i:
                        at.enter(i, {split: 2, wfree: 2, raw_in[0]: 16, raw_in[1]: 16})
                        for s in range(2):
                            at.step(raw_in[s], 16)
                            pool.wait_ge(raw_in[s].sem, at.value(raw_in[s]))
                            pool.wait_ge(wfree.sem, at.value(wfree, -1))
                            at.step(wfree)
                            pool.tensor_tensor(wh[:, s, :], raw[:, s, :], ones[:, 0:1].to_broadcast([P, TW]), ALU.mult)
                            pool.drain()
                            pool.tensor_tensor(wl[:, s, :], raw[:, s, :], wh[:, s, :].bitcast(F32),
                                               ALU.subtract).then_inc(split.sem, 1)
                            at.step(split)
                        at.leave(n // 2)

                split_tiles(2)
                sums_x()
                split_tiles(NZ)
                for t in range(NB + 1):
                    at.step(mix_free)
                    pool.wait_ge(mix_free.sem, at.value(mix_free))
                    w = P if t < NB else NS
                    uu = z[:, Z_U:Z_U + 4, t * P:t * P + w]
                    pool.tensor_tensor(uu, uu, gt[:, t % 2, :, 0:w], ALU.mult).then_inc(gated.sem, 1)
                pool.drain()
                for k in range(4):
                    pool.tensor_tensor(hh[:, 4 + k, :], z[:, Z_U + k, :], ones[:, 0:1].to_broadcast([P, TOK]), ALU.mult)
                    pool.drain()
                    ins = pool.tensor_tensor(hl[:, 4 + k, :], z[:, Z_U + k, :], hh[:, 4 + k, :].bitcast(F32),
                                             ALU.subtract)
                ins.then_inc(gate_done.sem, 1)
                at.step(qrd_new)
                for c in range(QUADS * CHUNKS):
                    quad, s = c // CHUNKS, c % 4
                    if c == 0:
                        pool.wait_ge(qrd_new.sem, at.value(qrd_new))
                    if c >= 4:
                        pool.wait_ge(cache_free.sem, at.value(cache_free, c - 3))
                    if c == 0 or c >= 4:
                        pool.tensor_tensor(marks[:, c:c + 1], ones[:, 0:1], ones[:, 0:1], ALU.mult)
                    for b in range(QB):
                        col = (quad * QB + b) * CHUNKS + c % CHUNKS
                        at_rows = bass.IndirectOffsetOnAxis(ap=crows[:, col:col + 1], axis=0)
                        pool.indirect_dma_start(cks[s][:, b].rearrange("p r c -> p (r c)"), None, cache_c,
                                                at_rows).then_inc(cache_in[s].sem, 16)
                        at_rows = bass.IndirectOffsetOnAxis(ap=crows[:, col:col + 1], axis=0)
                        pool.indirect_dma_start(rks[s][:, b].rearrange("p r c -> p (r c)"), None, cache_k,
                                                at_rows).then_inc(cache_in[s].sem, 16)
                split_tiles(KD)
                at.step(sq_full, 2 + 1 + 4 + KD)
                sums_x()
                split_tiles(TILES_LAYER - NZ - 2 - KD)
                at.done()
            at = Pos(DEPTH)
            sums_x()

        @block.scalar
        def _(act):
            for k in range(X_SP, KD):
                act.dma_start(x[:, k, :], xT[k]).then_inc(s_x[k], 16)
            act.wait_ge(s_init, 2)
            act.wait_ge(s_first, 32)

            def squares(tiles, ready=None):
                for k, t in enumerate(tiles):
                    if ready is not None:
                        ready(k)
                    n = at.k.get(sq_full, 0)
                    act.wait_ge(sq_free.sem, at.value(sq_free, 0 if n == SQ_TILES else -1))
                    at.step(sq_free)
                    act.activation(tmp[n % SQ_TILES % 2][:, :], t, ACT.Square).then_inc(sq_full.sem, 1)
                    at.step(sq_full)

            def roots(n, r):
                for g in range(NG):
                    at.step(mean_full)
                    act.wait_ge(mean_full.sem, at.value(mean_full))
                    act.activation(r[:, cols(g)], ps[6 + g % 2][:, 0:GW], ACT.Ln, bias=eps[:, 0:1],
                                   scale=1.0 / n).then_inc(mean_read.sem, 1)
                    at.step(mean_read)
                act.drain()
                act.activation(r[:, :], r[:, :], ACT.Exp, scale=-0.5).then_inc(root_full.sem, 1)
                at.step(root_full)

            def high_h(gain):
                for k in range(KD):
                    act.wait_ge(x_new.sem, at.value(x_new, -KD + k + 1))
                    act.activation(hh[:, k, :], x[:, k, :], ACT.Copy, scale=gain[:, k:k + 1]).then_inc(hh_new.sem, 1)
                    at.step(hh_new)
                    squares([x[:, k, :]])

            at = Pos(0)
            act.wait_ge(pre_in.sem, at.value(pre_in))
            high_h(gpre)
            with act.Fori(0, DEPTH) as l:
                at = Pos(l, {hh_new: KD, sq_full: KD, sq_free: KD})
                at.step(small_in, 16)
                act.wait_ge(small_in.sem, at.value(small_in))
                roots(D, rinv)
                at.step(x_stored, 16)
                for first, n in ((Z_Q, 2), (Z_C, 1), (Z_V, 4)):
                    act.wait_ge(acc_free.sem, at.value(acc_free, first + n))
                    squares([z[:, first + k, :] for k in range(n)])
                    if first == Z_Q:
                        act.wait_ge(x_stored.sem, at.value(x_stored))
                    roots(n * P, rin2)

                def load_head(h, e):
                    act.dma_start(wq[:, e], wuq[l, h]).then_inc(wqk_in.sem, 16)
                    act.dma_start(wk[:, e, :], wuk[l, h]).then_inc(wqk_in.sem, 16)
                    at.step(wqk_in, 32)

                def take_q(g):
                    at.step(q_full)
                    act.wait_ge(q_full.sem, at.value(q_full))
                    act.activation(qn[0:NOPE, cols(g)], ps[7][0:NOPE, 0:GW], ACT.Copy,
                                   scale=SCALE).then_inc(qn_new.sem, 1)
                    at.step(qn_new)

                def take_abs(g, e):
                    at.step(abs_full)
                    act.wait_ge(abs_full.sem, at.value(abs_full))
                    act.activation(qa[:, e, cols(g)], ps[7][:, 0:GW], ACT.Copy).then_inc(qa_new.sem, 1)
                    at.step(qa_new)

                def keep_q(h4, e):
                    dst = qd[:, :, :].rearrange("p q (b n) -> p q b n", n=160)[:, :, :, bass.ds(h4, 4)]
                    act.activation(dst, qa[:, e, SEQ:TOK].rearrange("p (q b t) -> p q b t", q=QUADS, b=QB), ACT.Copy)

                def exps(j):
                    at.step(nmax)
                    act.wait_ge(nmax.sem, at.value(nmax))
                    n, s = (j + 1) * P, j % 4
                    act.activation(pr[:, s, 0:n], s_of(j), ACT.Exp, bias=stat[:, 32 + s:33 + s],
                                   accum_out=stat[:, 36 + s:37 + s]).then_inc(exped.sem, 1)
                    at.step(exped)

                def take_pt(j):
                    for n in range(1 if j < 4 else 2):
                        at.step(pt_full)
                        act.wait_ge(pt_full.sem, at.value(pt_full))
                        kb = min(4, j + 1 - 4 * n)
                        bank = 4 + (at.k[pt_full] - 1) % 2
                        src = ps[bank][:, 0:kb * P].rearrange("p (k n) -> p k n", k=kb)
                        act.activation(pts[j // 4][:, 4 * n:4 * n + kb, (j % 4) * P:(j % 4 + 1) * P], src,
                                       ACT.Copy).then_inc(pt_new.sem, 1)
                        at.step(pt_new)

                def take_o(tile, half_):
                    at.step(o_full)
                    act.wait_ge(o_full.sem, at.value(o_full))
                    dst = z[:, bass.ds(tile, 1), 512 * half_:512 * half_ + 512]
                    act.activation(dst, ps[6][:, :].rearrange("p (a n) -> p a n", a=1),
                                   ACT.Copy).then_inc(o_new.sem, 1)
                    at.step(o_new)

                def head(hp, e, more):
                    if more:
                        load_head(hp * 2 + (e + 1), 1 - e)
                    exps(2)
                    take_pt(0)
                    exps(3)
                    take_pt(1)
                    exps(4)
                    if more:
                        take_q(0)
                    take_pt(2)
                    take_pt(3)
                    if more:
                        take_q(1)
                    exps(5)
                    take_o(hp * 2 + (Z_O + e), 0)
                    if more:
                        take_q(2)
                    take_pt(4)
                    exps(6)
                    if more:
                        take_abs(0, 1 - e)
                    take_pt(5)
                    exps(7)
                    if more:
                        take_abs(1, 1 - e)
                    take_pt(6)
                    if more:
                        take_abs(2, 1 - e)
                        act.drain()
                        keep_q(hp * 8 + (4 * e + 4), 1 - e)
                        exps(0)
                        exps(1)
                    take_pt(7)
                    act.wait_ge(gate_done.sem, at.value(gate_done))
                    take_o(hp * 2 + (Z_O + e), 1)

                load_head(0, 0)
                for t in range(NB + 1):
                    m = P if t < NB else NS
                    at.step(ct_full)
                    act.wait_ge(ct_full.sem, at.value(ct_full))
                    act.activation(cn[0:m, t, :], ps[6 + t % 2][0:m, 0:CL + ROPE], ACT.Copy).then_inc(ct_free.sem, 1)
                    at.step(ct_free)

                def take_v(t):
                    m = P if t < NB else NS
                    at.step(vt_full)
                    act.wait_ge(vt_full.sem, at.value(vt_full))
                    if t >= 2:
                        act.wait_ge(mix_full.sem, at.value(mix_full, t - 1))
                    act.activation(vn[0:m, t % 2, :], ps[4 + t % 2][0:m, :], ACT.Copy).then_inc(vt_free.sem, 1)
                    at.step(vt_free)

                take_v(0)
                for t in range(NB + 1):
                    if t < NB:
                        take_v(t + 1)
                    if t in Q_AT:
                        take_q(Q_AT.index(t))
                    if t in ABS_AT:
                        take_abs(ABS_AT.index(t), 0)
                at.step(mix_full, NB + 1)
                at.step(gate_done)
                at.step(qd_zero)
                act.drain()
                act.wait_ge(qd_zero.sem, at.value(qd_zero))
                keep_q(0, 0)
                exps(0)
                exps(1)
                with act.Fori(0, HEADS // 2 - 1) as hp:
                    at.enter(hp, {wqk_in: 64, q_full: 6, qn_new: 6, abs_full: 6, qa_new: 6, nmax: 16, exped: 16,
                                  pt_full: 24, pt_new: 24, o_full: 4, o_new: 4})
                    head(hp, 0, True)
                    head(hp, 1, True)
                    at.leave(HEADS // 2 - 1)
                head(HEADS // 2 - 1, 0, True)
                head(HEADS // 2 - 1, 1, False)

                def d_exp(first=False):
                    at.step(dmax)
                    act.wait_ge(dmax.sem, at.value(dmax))
                    s = d_exp.n % 2
                    d_exp.n += 1
                    if not first:
                        act.activation(stat[:, 12 + s:13 + s], stat[:, 10 + (1 - s):11 + (1 - s)], ACT.Exp,
                                       bias=stat[:, 10 + s:11 + s], scale=-1.0)
                    w = NS if first else 512
                    act.activation(pd[:, 0:w], ps[5][:, 0:w], ACT.Exp, bias=stat[:, 10 + s:11 + s],
                                   accum_out=stat[:, 14 + s:15 + s]).then_inc(dexp.sem, 1)
                    at.step(dexp)

                def d_keys():
                    for b in (2, 3):
                        at.step(dct_full, 5 if b == 2 else 0)
                        act.wait_ge(dct_full.sem, at.value(dct_full, b - 4))
                        act.activation(ctt[b], ps[b][:, :], ACT.Copy).then_inc(dct_act.sem, 1)
                        at.step(dct_act)

                def d_pt(n):
                    at.step(dpt_full)
                    act.wait_ge(dpt_full.sem, at.value(dpt_full))
                    if n == 1:
                        act.activation(ptd[0:NS, 0, :], ps[6][0:NS, 0:P], ACT.Copy).then_inc(dpt_new.sem, 1)
                    else:
                        act.activation(ptd, ps[6][:, :].rearrange("p (r n) -> p r n", r=4),
                                       ACT.Copy).then_inc(dpt_new.sem, 1)
                    at.step(dpt_new)

                for quad in range(QUADS):
                    d_exp.n = 0
                    d_exp(True)
                    d_pt(1)
                    d_keys()
                    d_exp()
                    for c in range(1, CHUNKS):
                        d_keys()
                        d_pt(4)
                        d_exp()
                    d_pt(4)
                    at.step(ot_full)
                    act.wait_ge(ot_full.sem, at.value(ot_full))
                    dst = z[:, Z_O:Z_O + HEADS, SEQ + 16 * quad:SEQ + 16 * quad + 16].rearrange(
                        "p h (b t) -> p b h t", b=QB)
                    src = ps[6][:, 0:P].rearrange("p (b h t) -> p b h t", b=QB, h=HEADS)
                    for b in range(QB):
                        ins = act.activation(dst[:, b], src[:, b], ACT.Copy)
                    ins.then_inc(ol_new.sem, 1)
                    at.step(ol_new)
                for u in range(UNITS_UV):
                    at.step(acc_full)
                    act.wait_ge(acc_full.sem, at.value(acc_full, UNITS_IN))
                    act.activation(groups(hh[:, u, :]), acc(u), ACT.Copy).then_inc(ab_h.sem, 1)
                    at.step(ab_h)
                at.step(acc_full, UNITS_IN)

                for m in range(UNITS_OUT):
                    at.step(acc_full)
                    act.wait_ge(acc_full.sem, at.value(acc_full))
                    act.wait_ge(sq_free.sem, at.value(sq_free, -1))
                    at.step(sq_free)
                    sl = at.k.get(sq_full, 0) % 2
                    act.activation(groups(tmp[sl][:, :]), acc(m), ACT.Square).then_inc(sq_full.sem, 1)
                    at.step(sq_full)
                    act.activation(groups(z[:, m, :]), acc(m), ACT.Copy).then_inc(acc_free.sem, 1)
                    at.step(acc_free)
                roots(D, rinv)
                at.step(x_new, KD)
                high_h(gn[:, G_FFN_PRE:G_FFN_PRE + KD])
                roots(D, rinv)
                at.step(x_stored, 16)
                act.wait_ge(x_stored.sem, at.value(x_stored))
                def hidden():
                    for j in range(4):
                        at.step(act_new)
                        act.wait_ge(act_new.sem, at.value(act_new))
                        s = j % 2
                        act.activation(z[:, 10 + s, :], z[:, 8 + s, :], ACT.Square)
                        act.drain()
                        act.activation(hidh[:, j, :], z[:, 10 + s, :], ACT.Copy).then_inc(hid_h.sem, 1)
                        at.step(hid_h)

                with act.Fori(0, FB - 1) as i:
                    at.enter(i, {act_new: 4, hid_h: 4})
                    hidden()
                    at.leave(FB - 1)
                hidden()
                at.step(acc_full, FB * (UNITS_UP + UNITS_DOWN))

                def y_done(k):
                    at.step(y_new)
                    act.wait_ge(y_new.sem, at.value(y_new))

                squares([z[:, k, :] for k in range(KD)], y_done)
                roots(D, rinv)
                at.step(x_new, KD)
                at.step(pre_in, 16)
                act.wait_ge(pre_in.sem, at.value(pre_in))
                high_h(gpre)
                at.done()

        @block.vector
        def _(dve):
            dve.memset(stat[:, 26:27], 0.0).then_inc(acc_free.sem, 2)
            dve.memset(stat[:, 27:28], 0.0).then_inc(sq_free.sem, 2)
            dve.memset(stat[:, 61:62], 0.0).then_inc(o_new.sem, 1)
            dve.memset(stat[:, 62:63], 0.0).then_inc(qa_new.sem, 1)
            dve.wait_ge(s_first, 32)
            dve.tensor_scalar(crows[:, :], kpt[:, :], 32.0, cst[:, C_ROW:C_ROW + 1], ALU.mult, ALU.add)
            dve.drain()

            def low_h(k, gain):
                at.step(hh_new)
                dve.wait_ge(hh_new.sem, at.value(hh_new))
                dve.scalar_tensor_tensor(out=hl[:, k, :], in0=x[:, k, :], scalar=gain[:, k:k + 1],
                                         in1=hh[:, k, :].bitcast(F32), op0=ALU.mult,
                                         op1=ALU.subtract).then_inc(hl_new.sem, 1)
                at.step(hl_new)

            at = Pos(0)
            for k in range(KD):
                dve.wait_ge(s_x[k], 16)
                dve.memset(stat[:, 50 + k:51 + k], 0.0).then_inc(x_new.sem, 1)
            dve.wait_ge(pre_in.sem, at.value(pre_in))
            for k in range(KD):
                low_h(k, gpre)
            with dve.Fori(0, DEPTH) as l:
                at = Pos(l, {hh_new: KD, hl_new: KD})

                def accumulate(k):
                    sl = at.k.get(sq_full, 0) % 2
                    at.step(sq_full)
                    if k:
                        dve.drain()
                    dve.wait_ge(sq_full.sem, at.value(sq_full))
                    if k == 0:
                        dve.wait_ge(root_full.sem, at.value(root_full)) if at.k.get(root_full, 0) else None
                        ins = dve.tensor_copy(sacc[:, :], tmp[sl][:, :])
                    else:
                        ins = dve.tensor_tensor(sacc[:, :], sacc[:, :], tmp[sl][:, :], ALU.add)
                    ins.then_inc(sq_free.sem, 1)
                    at.step(sq_free)
                    return ins

                def sums(n):
                    for k in range(n):
                        accumulate(k)
                    finish_sums()

                def finish_sums():
                    dve.drain()
                    dve.memset(stat[:, 24:25], 0.0).then_inc(sum_full.sem, 1)
                    at.step(sum_full)

                def root():
                    at.step(root_full)
                    dve.wait_ge(root_full.sem, at.value(root_full))

                def new_x(xin, gain, next_gain):
                    root()
                    at.step(x_loaded, 16)
                    dve.wait_ge(x_loaded.sem, at.value(x_loaded))
                    for k in range(KD):
                        dve.tensor_tensor(z[:, k, :], z[:, k, :], rinv[:, :], ALU.mult)
                        dve.drain()
                        dve.scalar_tensor_tensor(out=x[:, k, :], in0=z[:, k, :], scalar=gn[:, gain + k:gain + k + 1],
                                                 in1=xin[:, k, :], op0=ALU.mult, op1=ALU.add).then_inc(x_new.sem, 1)
                        at.step(x_new)
                        if k > 1:
                            low_h(k - 1, next_gain)
                        if k == 0:
                            low_h(0, next_gain)
                    low_h(KD - 1, next_gain)
                    at.step(sq_full, KD)
                    at.step(sum_full)

                at.step(small_in, 16)
                dve.wait_ge(small_in.sem, at.value(small_in))
                at.step(sq_full, KD)
                at.step(sum_full)
                root()
                def take_z(*units):
                    for u in units:
                        at.step(acc_full)
                        dve.wait_ge(acc_full.sem, at.value(acc_full))
                        dve.tensor_tensor(groups(z[:, u, :]), acc(u), groups(rinv[:, :]),
                                          ALU.mult).then_inc(acc_free.sem, 1)
                        at.step(acc_free)

                def norm_z(first, n, gain):
                    root()
                    for k in range(n):
                        ins = dve.scalar_tensor_tensor(out=z[:, first + k, :], in0=z[:, first + k, :],
                                                       scalar=gn[:, gain + k:gain + k + 1], in1=rin2,
                                                       op0=ALU.mult, op1=ALU.mult)
                    ins.then_inc(zn_done.sem, 1)
                    at.step(zn_done)

                take_z(0, 1)
                sums(2)
                take_z(2)
                at.step(x_stored, 16)
                dve.wait_ge(x_stored.sem, at.value(x_stored))
                dve.memset(wd, 0.0).then_inc(wd_zero.sem, 1)
                at.step(wd_zero)
                take_z(3)
                norm_z(Z_Q, 2, G_Q)
                sums(1)
                take_z(4, 5)
                norm_z(Z_C, 1, G_C)
                dve.tensor_tensor(kr[:, 0, :], z[0:32, Z_K, :], trig[0:32, :], ALU.mult)
                dve.tensor_tensor(kr[:, 1, :], z[32:64, Z_K, :], trig[32:64, :], ALU.mult)
                dve.drain()
                dve.tensor_tensor(z[0:32, Z_K, :], kr[:, 0, :], kr[:, 1, :], ALU.add).then_inc(zn_done.sem, 1)
                at.step(zn_done)
                take_z(6)
                at.step(gate_in, gate_in.per)
                dve.wait_ge(gate_in.sem, at.value(gate_in))
                for g in range(GROUPS):
                    dve.tensor_tensor(ws[:, g, :], ws[:, g, :], tril, ALU.mult)
                for g in range(GROUPS):
                    ins = dve.tensor_tensor(wd[:, g, :], wd[:, g, :], cst[0:NS, C_WD:C_WD + NS], ALU.mult)
                ins.then_inc(ws_ready.sem, 1)
                at.step(ws_ready)
                take_z(7)
                sums(4)
                take_z(8, 9)
                norm_z(Z_V, 4, G_V)
                take_z(10, 11)
                dve.drain()

                def turn_q(g, e):
                    at.step(q_full)
                    dve.wait_ge(q_full.sem, at.value(q_full))
                    a, b = rt[0:32, 0:GW], rt[0:32, GW:2 * GW]
                    dve.tensor_tensor(a, ps[7][64:96, 0:GW], trig[64:96, cols(g)], ALU.mult)
                    dve.tensor_tensor(b, ps[7][96:128, 0:GW], trig[96:128, cols(g)], ALU.mult)
                    dve.drain()
                    dve.tensor_tensor(qp[0:32, e, cols(g)], a, b, ALU.add).then_inc(qp_new.sem, 1)
                    at.step(qp_new)
                    dve.drain()

                def keep_q(h4, e):
                    src = qp[0:32, e, SEQ:TOK].rearrange("p (q b t) -> p q b t", q=QUADS, b=QB)
                    for q in range(QUADS):
                        dve.tensor_copy(qr[:, q, :, bass.ds(h4, 4)], src[:, q])

                def maxima(j):
                    at.step(s_full)
                    dve.wait_ge(s_full.sem, at.value(s_full))
                    sc = s_of(j)
                    dve.tensor_tensor(sc[:, j * P:], sc[:, j * P:], tri, ALU.add)
                    dve.drain()
                    dve.tensor_reduce(stat[:, 32 + j % 4:33 + j % 4], sc, AX.X, ALU.max,
                                      negate=True).then_inc(nmax.sem, 1)
                    at.step(nmax)

                def normalise(j):
                    at.step(exped)
                    dve.wait_ge(exped.sem, at.value(exped))
                    dve.reciprocal(stat[:, 44 + j % 4:45 + j % 4], stat[:, 36 + j % 4:37 + j % 4])
                    dve.drain()
                    w = (j + 1) * P
                    dve.tensor_scalar(pr[:, j % 4, 0:w], pr[:, j % 4, 0:w], stat[:, 44 + j % 4:45 + j % 4], None,
                                      ALU.mult).then_inc(p_new.sem, 1)
                    at.step(p_new)

                def head(hp, e, more):
                    normalise(0)
                    normalise(1)
                    maxima(2)
                    maxima(3)
                    normalise(2)
                    maxima(4)
                    normalise(3)
                    if more:
                        turn_q(0, 1 - e)
                        turn_q(1, 1 - e)
                    maxima(5)
                    normalise(4)
                    if more:
                        turn_q(2, 1 - e)
                        keep_q(hp * 8 + (4 * e + 4), 1 - e)
                    normalise(5)
                    maxima(6)
                    normalise(6)
                    maxima(7)
                    normalise(7)
                    if more:
                        maxima(0)
                        maxima(1)

                for t in range(NB + 1):
                    at.step(mix_full)
                    dve.wait_ge(mix_full.sem, at.value(mix_full))
                    if t >= 2:
                        dve.wait_ge(gated.sem, at.value(gated, t - 1))
                    w = P if t < NB else NS
                    for a in range(2):
                        rows = slice(64 * a, 64 * a + 64)
                        src = psum[rows, 2 * (t % 2):2 * (t % 2) + 2, 0:4 * w].rearrange(
                            "p c (a e i) -> p c a e i", a=2, e=2)[:, :, :, a, :]
                        dst = gt[rows, t % 2, :, 0:w].rearrange("p (c a) i -> p c a i", c=2)
                        bias = bb[rows, :, :].rearrange("p (c a) i -> p c a i", c=2)
                        if t < NB:
                            ins = dve.tensor_tensor(dst, src, bias, ALU.add)
                        else:
                            for b in range(DB):
                                own = slice(DT * b, DT * b + DT)
                                ins = dve.tensor_tensor(dst[:, :, :, own], src[:, :, :, own], bias[:, :, :, 0:DT],
                                                        ALU.add)
                    ins.then_inc(mix_free.sem, 1)
                    at.step(mix_free)
                    if t in Q_AT:
                        turn_q(Q_AT.index(t), 0)
                at.step(gated, NB + 1)
                at.step(outs, 80)
                dve.drain()
                dve.wait_ge(outs.sem, at.value(outs))
                dve.wait_ge(gated.sem, at.value(gated))
                dve.memset(qd, 0.0)
                dve.memset(qrd, 0.0)
                dve.drain()
                dve.memset(stat[:, 25:26], 0.0).then_inc(qd_zero.sem, 1)
                at.step(qd_zero)
                keep_q(0, 0)
                maxima(0)
                maxima(1)
                with dve.Fori(0, HEADS // 2 - 1) as hp:
                    at.enter(hp, {q_full: 6, qp_new: 6, s_full: 16, nmax: 16, exped: 16, p_new: 16})
                    head(hp, 0, True)
                    head(hp, 1, True)
                    at.leave(HEADS // 2 - 1)
                head(HEADS // 2 - 1, 0, True)
                head(HEADS // 2 - 1, 1, False)
                dve.drain()
                for b in range(QB):
                    for q in range(QUADS):
                        ins = dve.tensor_copy(qrd[32 * b:32 * b + 32, q, 32 * b:32 * b + 32], qr[:, q, b, :])
                for b in range(QB):
                    ins = dve.tensor_copy(kn[32 * b:32 * b + 32, :], z[0:32, Z_K, SEQ:TOK])
                dve.drain()
                at.step(o_new, 2 * HEADS)
                dve.wait_ge(o_new.sem, at.value(o_new))
                dve.memset(stat[:, 25:26], 0.0).then_inc(qrd_new.sem, 1)
                at.step(qrd_new)
                dve.memset(wv, 0.0).then_inc(wv_zero.sem, 1)
                at.step(wv_zero)

                def d_max(first=False, quad=0):
                    at.step(ds_full)
                    dve.wait_ge(ds_full.sem, at.value(ds_full))
                    s = d_max.n % 2
                    d_max.n += 1
                    if first:
                        dve.tensor_tensor(ps[5][:, 0:NS], ps[5][:, 0:NS],
                                          cst[:, C_NEW + NS * quad:C_NEW + NS * quad + NS], ALU.add)
                        dve.drain()
                        dve.tensor_reduce(stat[:, 10 + s:11 + s], ps[5][:, 0:NS], AX.X, ALU.max,
                                          negate=True).then_inc(dmax.sem, 1)
                    else:
                        dve.tensor_reduce(stat[:, 22:23], ps[5][:, :], AX.X, ALU.max, negate=True)
                        dve.drain()
                        dve.tensor_tensor(stat[:, 10 + s:11 + s], stat[:, 22:23], stat[:, 10 + 1 - s:11 + 1 - s],
                                          ALU.min).then_inc(dmax.sem, 1)
                    at.step(dmax)

                def d_keys(s):
                    at.step(cache_in[s], 32 * QB)
                    dve.wait_ge(cache_in[s].sem, at.value(cache_in[s]))
                    dve.tensor_copy(rk2, rks[s].rearrange("p b r c -> p r b c")).then_inc(rk_new.sem, 1)
                    at.step(rk_new)
                    for b in (0, 1, 4):
                        at.step(dct_full, 5 if b == 0 else 0)
                        dve.wait_ge(dct_full.sem, at.value(dct_full, b - 4))
                        dve.tensor_copy(ctt[b] if b < 4 else rtt, ps[b][:, :]).then_inc(dct_dve.sem, 1)
                        at.step(dct_dve)

                def d_sum():
                    at.step(dexp)
                    dve.wait_ge(dexp.sem, at.value(dexp))
                    s = d_sum.n % 2
                    d_sum.n += 1
                    dve.scalar_tensor_tensor(out=stat[:, 23:24], in0=stat[:, 23:24], scalar=stat[:, 12 + s:13 + s],
                                             in1=stat[:, 14 + s:15 + s], op0=ALU.mult, op1=ALU.add)
                    dve.tensor_copy(stat[:, 4 + 2 + s:4 + 3 + s], stat[:, 12 + s:13 + s])
                    dve.drain()

                def d_out():
                    at.step(do_full)
                    dve.wait_ge(do_full.sem, at.value(do_full))
                    s = d_out.n % 2
                    d_out.n += 1
                    for b in range(QB):
                        r = slice(32 * b, 32 * b + 32)
                        ins = dve.scalar_tensor_tensor(out=oacc[r, :], in0=oacc[r, :], scalar=stat[r, 6 + s:7 + s],
                                                       in1=ps[7][r, P * b:P * b + P], op0=ALU.mult, op1=ALU.add)
                    ins.then_inc(do_free.sem, 1)
                    at.step(do_free)
                    dve.drain()

                for quad in range(QUADS):
                    d_max.n = 0
                    d_sum.n = d_out.n = 1
                    d_max(True, quad)
                    at.step(dexp)
                    dve.wait_ge(dexp.sem, at.value(dexp))
                    dve.tensor_copy(stat[:, 23:24], stat[:, 14:15])
                    dve.drain()
                    at.step(do_full)
                    dve.wait_ge(do_full.sem, at.value(do_full))
                    dve.tensor_copy(oacc, ps[7][:, 0:P]).then_inc(do_free.sem, 1)
                    at.step(do_free)
                    dve.drain()
                    d_keys(0)
                    d_max()
                    for c in range(1, CHUNKS):
                        d_keys(c % 4)
                        d_sum()
                        if c >= 2:
                            d_out()
                        d_max()
                    d_sum()
                    d_out()
                    d_out()
                    dve.reciprocal(stat[:, 22:23], stat[:, 23:24])
                    dve.drain()
                    dve.tensor_scalar(oacc, oacc, stat[:, 22:23], None, ALU.mult).then_inc(on_new.sem, 1)
                    at.step(on_new)
                    at.step(ot_full)
                    dve.wait_ge(ot_full.sem, at.value(ot_full))

                for u in range(UNITS_UV):
                    at.step(ab_h)
                    dve.wait_ge(ab_h.sem, at.value(ab_h))
                    dve.tensor_tensor(groups(hl[:, u, :]), acc(u), groups(hh[:, u, :]).bitcast(F32),
                                      ALU.subtract).then_inc(acc_free.sem, 1)
                    at.step(acc_free)
                    at.step(acc_full)
                    dve.drain()
                    dve.memset(stat[:, 25:26], 0.0).then_inc(ab_l.sem, 1)
                    at.step(ab_l)
                sums(UNITS_OUT)
                at.step(acc_full, UNITS_OUT)
                at.step(acc_free, UNITS_OUT)
                new_x(x, G_MIX_POST, gn[:, G_FFN_PRE:G_FFN_PRE + KD])
                root()

                def block_of(first, last):
                    def low(j):
                        at.step(hid_h)
                        dve.wait_ge(hid_h.sem, at.value(hid_h))
                        dve.tensor_tensor(hidl[:, j, :], z[:, 10 + j % 2, :], hidh[:, j, :].bitcast(F32),
                                          ALU.subtract).then_inc(hid_l.sem, 1)
                        at.step(hid_l)

                    for j in range(4):
                        at.step(acc_full)
                        dve.wait_ge(acc_full.sem, at.value(acc_full))
                        dve.scalar_tensor_tensor(out=groups(z[:, 8 + j % 2, :]), in0=acc(j), scalar=0.0,
                                                 in1=groups(rinv[:, :]), op0=ALU.max,
                                                 op1=ALU.mult).then_inc(acc_free.sem, 1)
                        at.step(acc_free)
                        dve.drain()
                        dve.memset(stat[:, 25:26], 0.0).then_inc(act_new.sem, 1)
                        at.step(act_new)
                        if j > 0:
                            low(j - 1)
                    low(3)
                    for m in range(UNITS_DOWN):
                        at.step(acc_full)
                        dve.wait_ge(acc_full.sem, at.value(acc_full))
                        if first:
                            ins = dve.tensor_copy(groups(z[:, m, :]), acc(m))
                        else:
                            ins = dve.tensor_tensor(groups(z[:, m, :]), acc(m), groups(z[:, m, :]), ALU.add)
                        ins.then_inc(acc_free.sem, 1)
                        at.step(acc_free)
                        if last:
                            dve.drain()
                            dve.memset(stat[:, 25:26], 0.0).then_inc(y_new.sem, 1)
                            at.step(y_new)
                            if m:
                                accumulate(m - 1)
                    dve.drain()

                block_of(True, False)
                with dve.Fori(0, FB - 2) as i:
                    at.enter(i, {acc_full: 12, acc_free: 12, act_new: 4, hid_h: 4, hid_l: 4})
                    block_of(False, False)
                    at.leave(FB - 2)
                block_of(False, True)
                accumulate(KD - 1)
                finish_sums()
                at.step(pre_in, 16)
                dve.wait_ge(pre_in.sem, at.value(pre_in))
                new_x(x2, G_FFN_POST, gpre)
                at.k[sq_full] -= KD
                at.k[sum_full] -= 1
                dve.tensor_scalar(crows[:, :], crows[:, :], float(N_PHYS * 32), None, ALU.add)
                dve.drain()
                at.done()

        @block.tensor
        def _(pe):
            pe.wait_ge(s_first, 32)
            pe.wait_ge(s_init, 2)
            with pe.Fori(0, DEPTH) as l:
                at = Pos(l)

                def take_tile():
                    at.step(split)
                    pe.wait_ge(split.sem, at.value(split))

                held = [False]

                def release(ins):
                    if held[0]:
                        ins.then_inc(wfree.sem, 1)
                        at.step(wfree)
                        held[0] = False

                def release_now():
                    pe.wait_ge(acc_full.sem, at.value(acc_full))
                    pe.sem_inc(wfree.sem, 1)
                    at.step(wfree)
                    held[0] = False

                def dense(s, w0, kk, mh, ml, u, last_of_tile, ready=None):
                    at.step(acc_free)
                    pe.wait_ge(acc_free.sem, at.value(acc_free, -2))
                    for k in range(kk):
                        if ready is not None:
                            ready(k)
                        o = w0(k)
                        for n, (w, m) in enumerate(((wh, mh), (wh, ml), (wl, mh))):
                            for g in range(NG):
                                ins = pe.matmul(bank3(u, g), w[:, s, o:o + P], m[:, k, cols(g)],
                                                start=(k == 0 and n == 0), stop=(k == kk - 1 and n == 2))
                                release(ins)
                    ins.then_inc(acc_full.sem, 1)
                    at.step(acc_full)
                    held[0] = last_of_tile

                def dense_pair(ready):
                    take_tile()
                    take_tile()
                    at.step(acc_free, 2)
                    pe.wait_ge(acc_free.sem, at.value(acc_free, -2))
                    for k in range(KD):
                        ready(k)
                        for u in range(2):
                            for n, (w, m) in enumerate(((wh, hh), (wh, hl), (wl, hh))):
                                for g in range(NG):
                                    ins = pe.matmul(bank3(u, g), w[:, u, k * P:k * P + P], m[:, k, cols(g)],
                                                    start=(k == 0 and n == 0), stop=(k == KD - 1 and n == 2))
                                    release(ins)
                            if k == KD - 1:
                                ins.then_inc(acc_full.sem, 1)
                                at.step(acc_full)
                                held[0] = True

                def means():
                    at.step(sum_full)
                    pe.wait_ge(sum_full.sem, at.value(sum_full))
                    for g in range(NG):
                        if g == 2:
                            pe.wait_ge(mean_read.sem, at.value(mean_read, 1))
                        pe.matmul(ps[6 + g % 2][:, 0:GW], ones[:, :], sacc[:, cols(g)],
                                  start=True, stop=True).then_inc(mean_full.sem, 1)
                        at.step(mean_full)
                    at.step(mean_read, NG)

                def hl_ready(k):
                    at.step(hl_new)
                    pe.wait_ge(hl_new.sem, at.value(hl_new))

                dense_pair(hl_ready)
                means()
                for u in range(2, UNITS_IN):
                    take_tile()
                    dense(u % 2, lambda k: k * P, KD, hh, hl, u, True)
                    if u in (3, 5, 9):
                        means()
                release_now()
                at.step(zn_done, 4)
                pe.wait_ge(zn_done.sem, at.value(zn_done))
                for t in range(NB + 1):
                    m = P if t < NB else NS
                    if t >= 2:
                        pe.wait_ge(ct_free.sem, at.value(ct_free, t - 1))
                    tk = slice(t * P, t * P + m)
                    pe.transpose(ps[6 + t % 2][0:m, 0:CL], z[:, Z_C, tk], ident)
                    pe.transpose(ps[6 + t % 2][0:m, CL:CL + ROPE], z[0:ROPE, Z_K, tk],
                                 ident[0:ROPE, 0:ROPE]).then_inc(ct_full.sem, 1)
                    at.step(ct_full)
                at.step(ct_free, NB + 1)

                def turn_v(t):
                    m = P if t < NB else NS
                    if t >= 2:
                        pe.wait_ge(vt_free.sem, at.value(vt_free, t - 1))
                    for i in range(4):
                        ins = pe.transpose(ps[4 + t % 2][0:m, i * P:(i + 1) * P], z[:, Z_V + i, t * P:t * P + m], ident)
                    ins.then_inc(vt_full.sem, 1)
                    at.step(vt_full)

                def mix(t):
                    pe.wait_ge(vt_free.sem, at.value(vt_free, t + 1))
                    if t >= 2:
                        pe.wait_ge(mix_free.sem, at.value(mix_free, t - 1))
                    m = P if t < NB else NS
                    w = ws if t < NB else wd
                    for a in range(4):
                        ins = pe.matmul(ps[2 * (t % 2) + a // 2][:, (a % 2) * 2 * m:(a % 2) * 2 * m + 2 * m],
                                        vn[0:m, t % 2, a * P:(a + 1) * P], w[:, 2 * a:2 * a + 2, :],
                                        start=True, stop=True)
                    ins.then_inc(mix_full.sem, 1)
                    at.step(mix_full)

                def scores(j, e, done):
                    if done is not None:
                        pe.wait_ge(exped.sem, at.value(exped, done))
                    n = (j + 1) * P
                    for c in range((n + 511) // 512):
                        w = min(512, n - 512 * c)
                        bank = s_of(j)[:, 512 * c:512 * c + w]
                        pe.matmul(bank, qa[:, e, j * P:(j + 1) * P], z[:, Z_C, 512 * c:512 * c + w],
                                  start=True, stop=False)
                        ins = pe.matmul(bank, qp[0:ROPE, e, j * P:(j + 1) * P], z[0:ROPE, Z_K, 512 * c:512 * c + w],
                                        start=False, stop=True)
                    ins.then_inc(s_full.sem, 1)
                    at.step(s_full)

                def turn_p(j):
                    at.step(p_new)
                    pe.wait_ge(p_new.sem, at.value(p_new))
                    for n in range(1 if j < 4 else 2):
                        bank = 4 + at.k.get(pt_full, 0) % 2
                        if at.k.get(pt_full, 0) - turn_p.first >= 2:
                            pe.wait_ge(pt_new.sem, at.value(pt_new, at.k[pt_full] - at.k.get(pt_new, 0) - 1))
                        for kb in range(4 * n, min(j + 1, 4 * n + 4)):
                            ins = pe.transpose(ps[bank][:, (kb % 4) * P:(kb % 4 + 1) * P],
                                               pr[:, j % 4, kb * P:(kb + 1) * P], ident)
                        ins.then_inc(pt_full.sem, 1)
                        at.step(pt_full)

                def values(sb_):
                    at.step(pt_new, 4 if sb_ == 0 else 8)
                    pe.wait_ge(pt_new.sem, at.value(pt_new))
                    pe.wait_ge(o_new.sem, at.value(o_new))
                    at.step(o_new)
                    nk = 4 * sb_ + 4
                    for kb in range(nk):
                        q0 = max(0, kb - 4 * sb_) * P
                        ins = pe.matmul(ps[6][:, q0:512], cn[:, kb, 0:CL], pts[sb_][:, kb, q0:512],
                                        start=(kb == 0), stop=(kb == nk - 1))
                    ins.then_inc(o_full.sem, 1)
                    at.step(o_full)

                def make_q(g, e):
                    if g == 0:
                        at.step(wqk_in, 32)
                        pe.wait_ge(wqk_in.sem, at.value(wqk_in))
                        pe.wait_ge(qa_new.sem, at.value(qa_new))
                    else:
                        pe.wait_ge(qn_new.sem, at.value(qn_new, g))
                        pe.wait_ge(qp_new.sem, at.value(qp_new, g))
                    for k in range(2):
                        ins = pe.matmul(ps[7][:, 0:GW], wq[:, e, k, :], z[:, Z_Q + k, cols(g)],
                                        start=(k == 0), stop=(k == 1))
                    ins.then_inc(q_full.sem, 1)
                    at.step(q_full)

                def make_abs(g, e):
                    if g == 0:
                        at.step(qn_new, NG)
                        at.step(qp_new, NG)
                        pe.wait_ge(qn_new.sem, at.value(qn_new))
                        pe.wait_ge(qp_new.sem, at.value(qp_new))
                    else:
                        pe.wait_ge(qa_new.sem, at.value(qa_new, g))
                    pe.matmul(ps[7][:, 0:GW], wk[:, e, :], qn[0:NOPE, cols(g)],
                              start=True, stop=True).then_inc(abs_full.sem, 1)
                    at.step(abs_full)
                    if g == NG - 1:
                        at.step(qa_new, NG)

                def first_scores(e, done):
                    pe.wait_ge(qa_new.sem, at.value(qa_new))
                    scores(0, e, done)
                    scores(1, e, None)

                def head(e, more):
                    turn_p.first = at.k.get(pt_full, 0)
                    scores(2, e, 1)
                    scores(3, e, None)
                    turn_p(0)
                    turn_p(1)
                    scores(4, e, 2)
                    if more:
                        make_q(0, 1 - e)
                    turn_p(2)
                    turn_p(3)
                    if more:
                        make_q(1, 1 - e)
                    scores(5, e, 4)
                    values(0)
                    if more:
                        make_q(2, 1 - e)
                    turn_p(4)
                    scores(6, e, 5)
                    if more:
                        make_abs(0, 1 - e)
                    turn_p(5)
                    scores(7, e, 6)
                    if more:
                        make_abs(1, 1 - e)
                    turn_p(6)
                    if more:
                        make_abs(2, 1 - e)
                        first_scores(1 - e, 7)
                    turn_p(7)
                    values(1)
                    at.step(exped, NB)

                at.step(ws_ready)
                pe.wait_ge(ws_ready.sem, at.value(ws_ready))
                pe.wait_ge(ct_free.sem, at.value(ct_free))
                pe.wait_ge(acc_free.sem, at.value(acc_free))
                turn_v(0)
                for t in range(NB + 1):
                    if t < NB:
                        turn_v(t + 1)
                    mix(t)
                    if t in Q_AT:
                        make_q(Q_AT.index(t), 0)
                    if t in ABS_AT:
                        make_abs(ABS_AT.index(t), 0)
                at.step(vt_free, NB + 1)
                at.step(mix_free, NB + 1)
                pe.wait_ge(mix_free.sem, at.value(mix_free))
                first_scores(0, None)
                with pe.Fori(0, HEADS // 2 - 1) as hp:
                    at.enter(hp, {wqk_in: 64, q_full: 6, qn_new: 6, qp_new: 6, abs_full: 6, qa_new: 6, s_full: 16,
                                  exped: 16, p_new: 16, pt_full: 24, pt_new: 24, o_full: 4, o_new: 4})
                    head(0, True)
                    head(1, True)
                    at.leave(HEADS // 2 - 1)
                head(0, True)
                head(1, False)

                at.step(qrd_new)
                pe.wait_ge(qrd_new.sem, at.value(qrd_new))

                def q_of(quad, b):
                    return qd[:, quad, b * P:(b + 1) * P]

                def d_turn(s):
                    at.step(cache_in[s], 32 * QB)
                    pe.wait_ge(cache_in[s].sem, at.value(cache_in[s]))
                    for b in range(QB + 1):
                        if at.k.get(dct_full, 0) > 4:
                            if b in (2, 3):
                                pe.wait_ge(dct_act.sem, at.value(dct_act, b - 3))
                            else:
                                pe.wait_ge(dct_dve.sem, at.value(dct_dve, {0: -2, 1: -1, 4: 0}[b]))
                        if b == QB:
                            at.step(rk_new)
                            pe.wait_ge(rk_new.sem, at.value(rk_new))
                        for r in range(4):
                            src = cks[s][:, b, r, :] if b < QB else rk2[:, r, :, :].rearrange("p b c -> p (b c)")
                            ins = pe.transpose(ps[b][:, r * P:(r + 1) * P], src, ident)
                        ins.then_inc(dct_full.sem, 1)
                        at.step(dct_full)
                    at.step(dct_act, 2)
                    at.step(dct_dve, 3)

                def d_scores(quad):
                    pe.wait_ge(dexp.sem, at.value(dexp))
                    pe.wait_ge(dct_act.sem, at.value(dct_act))
                    pe.wait_ge(dct_dve.sem, at.value(dct_dve))
                    for b in range(QB):
                        pe.matmul(ps[5][:, :], q_of(quad, b), ctt[b], start=(b == 0), stop=False)
                    pe.matmul(ps[5][:, :], qrd[:, quad, :], rtt, start=False, stop=True).then_inc(ds_full.sem, 1)
                    at.step(ds_full)

                def d_turn_p():
                    at.step(dexp)
                    pe.wait_ge(dexp.sem, at.value(dexp))
                    for r in range(4):
                        ins = pe.transpose(ps[6][:, r * P:(r + 1) * P], pd[:, r * P:(r + 1) * P], ident)
                    ins.then_inc(dpt_full.sem, 1)
                    at.step(dpt_full)

                def d_values(s):
                    at.step(dpt_new)
                    pe.wait_ge(dpt_new.sem, at.value(dpt_new))
                    pe.wait_ge(do_free.sem, at.value(do_free))
                    at.step(do_free)
                    for r in range(4):
                        ins = pe.matmul(ps[7][:, :], ptd[:, r, :], cks[s][:, :, r, :], start=(r == 0), stop=(r == 3))
                    ins.then_inc(do_full.sem, 1)
                    at.step(do_full)
                    pe.wait_ge(do_full.sem, at.value(do_full))
                    pe.sem_inc(cache_free.sem, 1)
                    at.step(cache_free)

                for quad in range(QUADS):
                    if quad:
                        pe.wait_ge(dexp.sem, at.value(dexp))
                    for b in range(QB):
                        pe.matmul(ps[5][:, 0:NS], q_of(quad, b), z[:, Z_C, SEQ:TOK], start=(b == 0), stop=False)
                    pe.matmul(ps[5][:, 0:NS], qrd[:, quad, :], kn, start=False, stop=True).then_inc(ds_full.sem, 1)
                    at.step(ds_full)
                    at.step(dexp)
                    pe.wait_ge(dexp.sem, at.value(dexp))
                    if quad:
                        pe.wait_ge(ol_new.sem, at.value(ol_new))
                        pe.wait_ge(do_free.sem, at.value(do_free))
                    pe.transpose(ps[6][0:NS, 0:P], pd[:, 0:NS], ident).then_inc(dpt_full.sem, 1)
                    at.step(dpt_full)
                    at.step(dpt_new)
                    pe.wait_ge(dpt_new.sem, at.value(dpt_new))
                    pe.matmul(ps[7][:, 0:P], ptd[0:NS, 0, :], cn[0:NS, NB, 0:CL], start=True,
                              stop=True).then_inc(do_full.sem, 1)
                    at.step(do_full)
                    at.step(do_free)
                    d_turn(0)
                    d_scores(quad)
                    for c in range(1, CHUNKS):
                        d_turn(c % 4)
                        if c >= 2:
                            d_values((c - 2) % 4)
                        d_turn_p()
                        d_scores(quad)
                    d_values((CHUNKS - 2) % 4)
                    d_turn_p()
                    d_values((CHUNKS - 1) % 4)
                    at.step(on_new)
                    pe.wait_ge(on_new.sem, at.value(on_new))
                    pe.transpose(ps[6][:, 0:P], oacc, ident).then_inc(ot_full.sem, 1)
                    at.step(ot_full)
                    at.step(ol_new)
                pe.wait_ge(ol_new.sem, at.value(ol_new))
                at.step(wv_in, 32)
                pe.wait_ge(wv_in.sem, at.value(wv_in))
                for u in range(UNITS_UV):
                    at.step(acc_free)
                    pe.wait_ge(acc_free.sem, at.value(acc_free, -2))
                    for e in range(2):
                        for g in range(NG):
                            ins = pe.matmul(bank3(u, g), wv[:, 2 * u + e, :], z[:, Z_O + 2 * u + e, cols(g)],
                                            start=(e == 0), stop=(e == 1))
                    ins.then_inc(acc_full.sem, 1)
                    at.step(acc_full)
                at.step(ab_l, UNITS_UV)
                pe.wait_ge(ab_l.sem, at.value(ab_l))
                at.step(gate_done)
                pe.wait_ge(gate_done.sem, at.value(gate_done))
                for u in range(2):
                    take_tile()
                    dense(u, lambda k: k * P, KD, hh, hl, u, True)
                with pe.Fori(1, UNITS_OUT // 2) as i:
                    at.enter(i - 1, {split: 2, wfree: 2, acc_free: 2, acc_full: 2})
                    for s in range(2):
                        take_tile()
                        dense(s, lambda k: k * P, KD, hh, hl, s, True)
                    at.leave(UNITS_OUT // 2 - 1)
                release_now()
                means()
                def up(j, ready=None):
                    take_tile()
                    dense(j % 2, lambda k: k * P, KD, hh, hl, j, True, ready)

                def down(m, ready=None):
                    if m % 2 == 0:
                        take_tile()
                    dense((m // 2) % 2, lambda k: k * 2 * P + (m % 2) * P, 4, hidh, hidl, m, m % 2 == 1, ready)

                def hid_ready(k):
                    at.step(hid_l)
                    pe.wait_ge(hid_l.sem, at.value(hid_l))

                dense_pair(hl_ready)
                means()
                for j in range(2, 4):
                    up(j)
                for m in range(UNITS_DOWN):
                    down(m, hid_ready if m == 0 else None)
                with pe.Fori(1, FB) as i:
                    at.enter(i - 1, {split: 8, wfree: 8, acc_free: 12, acc_full: 12, hid_l: 4})
                    for j in range(4):
                        up(j)
                    for m in range(UNITS_DOWN):
                        down(m, hid_ready if m == 0 else None)
                    at.leave(FB - 1)
                release_now()
                means()
                at.done()


def _constants():
    pos = np.concatenate([np.arange(SEQ), np.tile(PAST + np.arange(DT), DB)]).astype(np.float32)
    half = ROPE // 2
    freqs = np.power(np.float32(10000.0), (-np.arange(half, dtype=np.float32) / np.float32(half))).astype(np.float32)
    ang = (pos[:, None] * freqs[None, :]).astype(np.float32)
    cos, sin = np.cos(ang).T, np.sin(ang).T
    c = np.zeros((P, C_ALL), np.float32)
    for base in (0, 64):
        c[base:base + 32, 0:TOK] = np.concatenate([cos, cos])
        c[base + 32:base + 64, 0:TOK] = np.concatenate([-sin, sin])
    c[64:128, 0:TOK] *= np.float32(SCALE)
    i = np.arange(P)
    c[:, C_ID:C_ID + P] = np.eye(P)
    c[:, C_TRI:C_TRI + P] = np.where(i[None, :] <= i[:, None], 0.0, NEG)
    c[:, C_TRIL:C_TRIL + P] = i[None, :] >= i[:, None]
    j = np.arange(NS)
    for quad in range(QUADS):
        own = (j[None, :] // DT == quad * QB + i[:, None] // 32) & (j[None, :] % DT <= i[:, None] % DT)
        c[:, C_NEW + NS * quad:C_NEW + NS * quad + NS] = np.where(own, 0.0, NEG)
    c[:, C_ROW] = i % 32
    c[0:NS, C_WD:C_WD + NS] = (j[:, None] // DT == j[None, :] // DT) & (j[:, None] % DT <= j[None, :] % DT)
    return c


def kernel(**inputs):
    import concourse.bacc as _bacc
    from concourse.bass_utils import run_bass_kernel_spmd as _run

    a = {k: np.asarray(v) for k, v in inputs.items()}
    x = np.concatenate([a["x_prompt"].reshape(SEQ, D), a["x_sample"].reshape(NS, D)])
    w = a["w_in"]
    s1, s2, s3, s4 = QL, QL + CL, QL + CL + ROPE, QL + CL + ROPE + GM
    half = ROPE // 2
    kpe = w[:, :, s2:s3]
    swp = np.concatenate([kpe[:, :, half:], kpe[:, :, :half]], axis=2)
    w = np.concatenate([w[:, :, :s2], kpe, swp, kpe, swp, w[:, :, s4:], w[:, :, s3:s4]], axis=2)

    def tiles(m, n):
        L, K, N = m.shape
        return m.reshape(L, K // P, P, N // n, n).transpose(0, 3, 2, 1, 4).reshape(L, N // n, P, -1)

    up = tiles(a["w_ff_up"], P).reshape(DEPTH, FB, 4, P, TW)
    dn = a["w_ff_down"].reshape(DEPTH * FB, FF // FB, D)
    dn = tiles(dn, 2 * P).reshape(DEPTH, FB, 4, P, TW)
    ff = np.concatenate([up, dn], axis=2).reshape(DEPTH, FB * 8, P, TW)
    stream = np.concatenate([tiles(w, P), tiles(a["w_out"], P), ff], axis=1)

    def col(g):
        return g.reshape(DEPTH, -1, P).transpose(0, 2, 1)

    gains = np.concatenate([col(a[n]) for n in ("norm_mix_pre", "norm_mix_post", "norm_ffn_pre", "norm_ffn_post",
                                                "q_norm", "kv_norm", "v_norm")], axis=2)
    pre = np.roll(gains[:, :, G_MIX_PRE:G_MIX_PRE + KD], -1, axis=0)
    q = a["w_uq"]
    qpe = q[..., NOPE:]
    q = np.concatenate([q, qpe[..., half:], qpe[..., :half]], axis=3)
    wuq = q.reshape(DEPTH, 2, P, HEADS, P).transpose(0, 3, 2, 1, 4)
    wuk = a["w_uk"].transpose(0, 2, 3, 1)
    wsp = a["w_spatial"].transpose(0, 3, 1, 2)
    bsp = np.repeat(a["b_spatial"].reshape(DEPTH, 4, 2, P).transpose(0, 2, 1, 3), 64, axis=1)
    arrays = {
        "xT": x.T.reshape(KD, P, TOK), "wst": stream, "gains": gains, "pre": pre, "wuq": wuq, "wuk": wuk, "wuv": a["w_uv"],
        "wsp": wsp, "bsp": bsp,
        "cache_c": a["cache_kv_latent"].reshape(DEPTH * N_PHYS * 32, 4 * CL),
        "cache_k": a["cache_k_rope"].reshape(DEPTH * N_PHYS * 32, 4 * ROPE),
        "pages": np.repeat(a["page_table"].reshape(DB * CHUNKS, 4).T, 32, axis=0), "consts": _constants(),
    }
    arrays = {k: np.ascontiguousarray(v) for k, v in arrays.items()}
    nc = _bacc.Bacc("TRN2", target_bir_lowering=False, num_devices=1)
    ins = [nc.dram_tensor(k, v.shape, mybir.dt.from_np(v.dtype), kind="ExternalInput").ap() for k, v in arrays.items()]
    shapes = {"yT": (KD, P, TOK), "o_cp": (DEPTH, NB, P, CL), "o_kp": (DEPTH, NB, P, ROPE), "o_cs": (DEPTH, NS, CL),
              "o_ks": (DEPTH, NS, ROPE), "o_vs": (DEPTH, NS, GM)}
    outs = [nc.dram_tensor(k, s, F32, kind="ExternalOutput").ap() for k, s in shapes.items()]
    spill = nc.dram_tensor("x_spill", (KD, P, TOK), F32, kind="Internal").ap()
    build(nc, *ins, *outs, spill)
    r = _run(nc, [arrays], core_ids=[0]).results[0]
    y = np.ascontiguousarray(r["yT"].reshape(D, TOK).T)
    return (y[:SEQ].reshape(1, SEQ, D), y[SEQ:].reshape(DB, DT, D),
            r["o_cp"].reshape(DEPTH, 1, NB, P, CL), r["o_kp"].reshape(DEPTH, 1, NB, P, ROPE),
            r["o_cs"].reshape(DEPTH, DB, DT, CL), r["o_ks"].reshape(DEPTH, DB, DT, ROPE),
            r["o_vs"].reshape(DEPTH, DB, DT, GM))
```
